# Optimizing a Trainium2 kernel written in Bass

```python
import math
import jax, jax.numpy as jnp
from jax import lax
import numpy as np

D_MODEL = 1024
BATCH = 1
SEQ = 1024
DEPTH = 1
DEC_BATCH = 8
DEC_SEQ = 16
PAST_LEN = 512

CHUNK = 64
N_HEADS = 8
HEAD_DIM = 64
ATTN_WIDTH = N_HEADS * HEAD_DIM
LRU_WIDTH = D_MODEL - ATTN_WIDTH
LRU_BLOCKS = 8
LRU_BLOCK_DIM = LRU_WIDTH // LRU_BLOCKS
CONV_W = 4
RGLRU_C = 8.0
D_FF = 4 * D_MODEL
Q_BLOCK = 128
EPS = 1e-6
ATTN_SCALE = 1.0 / math.sqrt(HEAD_DIM)
SPLITS = (ATTN_WIDTH, 2 * ATTN_WIDTH, 3 * ATTN_WIDTH, 3 * ATTN_WIDTH + N_HEADS,
          3 * ATTN_WIDTH + N_HEADS + LRU_WIDTH)
IN_WIDTH = 3 * ATTN_WIDTH + N_HEADS + 2 * LRU_WIDTH

kernel_name = "hymba_fox_rglru_streaming_step"

def rms_norm(x, g):
    xf = x.astype(jnp.float32)
    y = xf * lax.rsqrt(jnp.mean(xf * xf, axis=-1, keepdims=True) + EPS)
    return (y * g).astype(x.dtype)

def fox_attend(q, k, v, cq, ck, q_pos, k_pos):
    s = jnp.einsum('bqhd,bkhd->bhqk', q, k, preferred_element_type=jnp.float32) * ATTN_SCALE
    s = s + jnp.transpose(cq, (0, 2, 1))[:, :, :, None] - jnp.transpose(ck, (0, 2, 1))[:, :, None, :]
    mask = k_pos[None, :] <= q_pos[:, None]
    s = jnp.where(mask[None, None], s, -jnp.inf)
    p = jax.nn.softmax(s, axis=-1).astype(v.dtype)
    return jnp.einsum('bhqk,bkhd->bqhd', p, v)

def fox_prompt(q, k, v, logf):
    B, T, H, Dh = q.shape
    c = jnp.cumsum(logf, axis=1)
    nb = T // Q_BLOCK
    qb = jnp.transpose(q.reshape(B, nb, Q_BLOCK, H, Dh), (1, 0, 2, 3, 4))
    cqb = jnp.transpose(c.reshape(B, nb, Q_BLOCK, H), (1, 0, 2, 3))
    posb = jnp.arange(T, dtype=jnp.int32).reshape(nb, Q_BLOCK)
    kpos = jnp.arange(T, dtype=jnp.int32)

    def one_block(args):
        qi, cqi, pi = args
        return fox_attend(qi, k, v, cqi, c, pi, kpos)

    out = lax.map(one_block, (qb, cqb, posb))
    return jnp.transpose(out, (1, 0, 2, 3, 4)).reshape(B, T, H, Dh)

def fox_sample(q, k, v, logf, k_past, v_past, logf_past):
    P = k_past.shape[1]
    T = q.shape[1]
    k_all = jnp.concatenate([k_past.astype(k.dtype), k], axis=1)
    v_all = jnp.concatenate([v_past.astype(v.dtype), v], axis=1)
    c_all = jnp.cumsum(jnp.concatenate([logf_past.astype(jnp.float32), logf], axis=1), axis=1)
    q_pos = P + jnp.arange(T, dtype=jnp.int32)
    k_pos = jnp.arange(P + T, dtype=jnp.int32)
    return fox_attend(q, k_all, v_all, c_all[:, P:], c_all, q_pos, k_pos)

def causal_conv(x, buf, w, b):
    T = x.shape[1]
    xp = jnp.concatenate([buf.astype(x.dtype), x], axis=1)
    y = sum(xp[:, j:j + T] * w[j] for j in range(CONV_W)) + b
    return y.astype(x.dtype), xp[:, -(CONV_W - 1):]

def rg_lru(x, h0, w_ga, b_ga, w_gx, b_gx, lam):
    B, T, W = x.shape
    xb = x.reshape(B, T, LRU_BLOCKS, LRU_BLOCK_DIM)
    r = jax.nn.sigmoid((jnp.einsum('btnc,ncd->btnd', xb, w_ga).reshape(B, T, W) + b_ga).astype(jnp.float32))
    i = jax.nn.sigmoid((jnp.einsum('btnc,ncd->btnd', xb, w_gx).reshape(B, T, W) + b_gx).astype(jnp.float32))
    log_a = -RGLRU_C * r * jax.nn.softplus(-lam.astype(jnp.float32))
    a = jnp.exp(log_a)
    bterm = jnp.sqrt(-jnp.expm1(2.0 * log_a)) * (i * x.astype(jnp.float32))
    bterm = bterm.at[:, 0].add(a[:, 0] * h0.astype(jnp.float32))

    def combine(left, right):
        a1, b1 = left
        a2, b2 = right
        return a1 * a2, a2 * b1 + b2

    _, h = lax.associative_scan(combine, (a, bterm), axis=1)
    return h, h[:, -1]

def hybrid_layer(x, past, ln1, w_in, b_f, q_gain, k_gain, conv_w, conv_b, w_ga, b_ga,
                 w_gx, b_gx, lam, g_ao, g_lo, w_out, ln2, w_up, w_down):
    B, T, _ = x.shape
    h = rms_norm(x, ln1)
    proj = h @ w_in
    q, k, v, f, xr, yg = jnp.split(proj, SPLITS, axis=-1)
    q = rms_norm(q.reshape(B, T, N_HEADS, HEAD_DIM), q_gain)
    k = rms_norm(k.reshape(B, T, N_HEADS, HEAD_DIM), k_gain)
    v = v.reshape(B, T, N_HEADS, HEAD_DIM)
    logf = jax.nn.log_sigmoid((f + b_f).astype(jnp.float32))

    if past is None:
        attn = fox_prompt(q, k, v, logf)
        h0 = jnp.zeros((B, LRU_WIDTH), jnp.float32)
        conv_buf = jnp.zeros((B, CONV_W - 1, LRU_WIDTH), x.dtype)
    else:
        k_past, v_past, logf_past, h0, conv_buf = past
        attn = fox_sample(q, k, v, logf, k_past, v_past, logf_past)

    xc, new_conv = causal_conv(xr, conv_buf, conv_w, conv_b)
    hs, h_last = rg_lru(xc, h0, w_ga, b_ga, w_gx, b_gx, lam)
    lru_out = jax.nn.gelu(yg) * hs.astype(x.dtype)

    mixed = jnp.concatenate([rms_norm(attn.reshape(B, T, ATTN_WIDTH), g_ao),
                             rms_norm(lru_out, g_lo)], axis=-1)
    x = x + mixed @ w_out
    h2 = rms_norm(x, ln2)
    x = x + jnp.square(jax.nn.relu(h2 @ w_up)) @ w_down
    return x, (k, v, logf, h_last, new_conv)

def setup_inputs(seed: int = 0) -> dict:
    key = jax.random.key(seed)
    ks = jax.random.split(key, 32)
    f32 = jnp.float32
    nrm = lambda k, shape, s: jax.random.normal(k, shape, f32) * s
    u = jax.random.uniform(ks[14], (DEPTH, LRU_WIDTH), f32, 0.9, 0.999)
    return {
        "x_prompt": nrm(ks[0], (BATCH, SEQ, D_MODEL), 1.0),
        "x_sample": nrm(ks[1], (DEC_BATCH, DEC_SEQ, D_MODEL), 1.0),
        "cache_k": nrm(ks[2], (DEPTH, DEC_BATCH, PAST_LEN, N_HEADS, HEAD_DIM), 1.0),
        "cache_v": nrm(ks[3], (DEPTH, DEC_BATCH, PAST_LEN, N_HEADS, HEAD_DIM), 1.0),
        "cache_logf": jax.nn.log_sigmoid(3.0 + nrm(ks[4], (DEPTH, DEC_BATCH, PAST_LEN, N_HEADS), 1.0)),
        "state_h": nrm(ks[5], (DEPTH, DEC_BATCH, LRU_WIDTH), 0.5),
        "state_conv": nrm(ks[6], (DEPTH, DEC_BATCH, CONV_W - 1, LRU_WIDTH), 1.0),
        "ln1": 1.0 + nrm(ks[7], (DEPTH, D_MODEL), 0.02),
        "w_in": nrm(ks[8], (DEPTH, D_MODEL, IN_WIDTH), D_MODEL ** -0.5),
        "b_f": 3.0 + nrm(ks[9], (DEPTH, N_HEADS), 0.5),
        "q_gain": 1.0 + nrm(ks[10], (DEPTH, HEAD_DIM), 0.02),
        "k_gain": 1.0 + nrm(ks[11], (DEPTH, HEAD_DIM), 0.02),
        "conv_w": nrm(ks[12], (DEPTH, CONV_W, LRU_WIDTH), CONV_W ** -0.5),
        "conv_b": nrm(ks[13], (DEPTH, LRU_WIDTH), 0.02),
        "w_gate_a": nrm(ks[15], (DEPTH, LRU_BLOCKS, LRU_BLOCK_DIM, LRU_BLOCK_DIM), LRU_BLOCK_DIM ** -0.5),
        "b_gate_a": nrm(ks[16], (DEPTH, LRU_WIDTH), 0.1),
        "w_gate_x": nrm(ks[17], (DEPTH, LRU_BLOCKS, LRU_BLOCK_DIM, LRU_BLOCK_DIM), LRU_BLOCK_DIM ** -0.5),
        "b_gate_x": nrm(ks[18], (DEPTH, LRU_WIDTH), 0.1),
        "lru_lambda": jnp.log(u) - jnp.log1p(-u),
        "g_attn_out": 1.0 + nrm(ks[19], (DEPTH, ATTN_WIDTH), 0.02),
        "g_lru_out": 1.0 + nrm(ks[20], (DEPTH, LRU_WIDTH), 0.02),
        "w_out": nrm(ks[21], (DEPTH, D_MODEL, D_MODEL), D_MODEL ** -0.5),
        "ln2": 1.0 + nrm(ks[22], (DEPTH, D_MODEL), 0.02),
        "w_up": nrm(ks[23], (DEPTH, D_MODEL, D_FF), D_MODEL ** -0.5),
        "w_down": nrm(ks[24], (DEPTH, D_FF, D_MODEL), D_FF ** -0.5),
    }

def reference(x_prompt, x_sample, cache_k, cache_v, cache_logf, state_h, state_conv,
              ln1, w_in, b_f, q_gain, k_gain, conv_w, conv_b, w_gate_a, b_gate_a,
              w_gate_x, b_gate_x, lru_lambda, g_attn_out, g_lru_out, w_out, ln2, w_up, w_down):
    yp, ys = x_prompt, x_sample
    kp, vp, fp, hp, cp = [], [], [], [], []
    kss, vss, fss, hss, css = [], [], [], [], []
    for l in range(DEPTH):
        params = (ln1[l], w_in[l], b_f[l], q_gain[l], k_gain[l], conv_w[l], conv_b[l],
                  w_gate_a[l], b_gate_a[l], w_gate_x[l], b_gate_x[l], lru_lambda[l],
                  g_attn_out[l], g_lru_out[l], w_out[l], ln2[l], w_up[l], w_down[l])
        yp, (k1, v1, f1, h1, c1) = hybrid_layer(yp, None, *params)
        ys, (k2, v2, f2, h2, c2) = hybrid_layer(
            ys, (cache_k[l], cache_v[l], cache_logf[l], state_h[l], state_conv[l]), *params)
        kp.append(k1); vp.append(v1); fp.append(f1); hp.append(h1); cp.append(c1)
        kss.append(k2); vss.append(v2); fss.append(f2); hss.append(h2); css.append(c2)
    return (yp, ys,
            jnp.stack(kp), jnp.stack(vp), jnp.stack(fp), jnp.stack(hp), jnp.stack(cp),
            jnp.stack(kss), jnp.stack(vss), jnp.stack(fss), jnp.stack(hss), jnp.stack(css))


_drawn_inputs = setup_inputs


def setup_inputs(seed=0):
    import zlib

    import numpy as np

    out = dict(_drawn_inputs(seed))
    spreads = {}
    factors = {'q_gain': 5.587, 'k_gain': 2.759, 'g_attn_out': 5.538, 'g_lru_out': 5.747, 'ln2': 3.722}
    for name, (base, spread) in spreads.items():
        noise = np.random.default_rng([zlib.crc32(name.encode()), seed]).standard_normal(out[name].shape)
        drawn = base * np.exp(spread * noise) if base else spread * noise
        out[name] = __import__('jax').numpy.asarray(drawn.astype(out[name].dtype))
    for name, factor in factors.items():
        out[name] = (out[name] * factor).astype(out[name].dtype)
    return out
```

```python
from contextlib import ExitStack

import numpy as np

import concourse.bass as bass
from concourse import mybir

F32 = mybir.dt.float32
F32R = mybir.dt.float32r
BF16 = mybir.dt.bfloat16
ALU = mybir.AluOpType
ACT = mybir.ActivationFunctionType
AX_X = mybir.AxisListType.X

P = 128
D = 1024
SEQ = 1024
DEC_B = 8
DEC_T = 16
PAST = 512
H = 8
DH = 64
AW = H * DH
LW = D - AW
FF = 4 * D
CW = 4
EPS = 1e-6
T_ALL = SEQ + DEC_B * DEC_T
NT = T_ALL // P
KC = D // P
G = 3
GN = T_ALL // G
LC = LW // P
PAIRS = H // 2
MASKED = -(2.0 ** 100)
F_COL = 3 * AW
XR_COL = F_COL + H
YG_COL = XR_COL + LW
ROWS = 42
R_CONVW, R_CONVB, R_BGA, R_BGX, R_LAM, R_GAO, R_GLO, R_H0, R_CONV = 0, 4, 5, 6, 7, 8, 9, 10, 18
R_SP4, R_NSP4, R_HBGA, R_HBGX = 42, 43, 44, 45
PW = 46
KP = PAST // P
KEYS = PAST + P
FB = 256
NFB = FF // FB


def streaming_step(nc, x_prompt, x_sample, cache_k, cache_v, cache_logf, state_h, state_conv, ln1, w_in, b_f,
                   q_gain, k_gain, conv_w, conv_b, w_gate_a, b_gate_a, w_gate_x, b_gate_x, lru_lambda,
                   g_attn_out, g_lru_out, w_out, ln2, w_up, w_down,
                   y_prompt, y_sample, k_prompt, v_prompt, logf_prompt, h_prompt, conv_prompt,
                   k_sample, v_sample, logf_sample, h_sample, conv_sample):
    ctx = ExitStack()

    def sem(name):
        return ctx.enter_context(nc.semaphore(name))

    def sb(scope, name, shape, dt=F32):
        return scope.enter_context(nc.sbuf_tensor(name, shape, dt))

    h_hi = sb(ctx, "h_hi", [P, KC, T_ALL], F32R)
    h_lo = sb(ctx, "h_lo", [P, KC, T_ALL], F32R)
    mix = sb(ctx, "mix", [P, KC, T_ALL])
    ident = sb(ctx, "ident", [P, P])
    ones_col = sb(ctx, "ones_col", [P, 1])
    neg_half = sb(ctx, "neg_half", [P, 4])
    param = sb(ctx, "param", [P, LC, PW])
    x_ss = sb(ctx, "x_ss", [P, NT])
    x_ms = sb(ctx, "x_ms", [P, NT])
    x_rs = sb(ctx, "x_rs", [P, NT])

    h_keep = sb(ctx, "h_keep", [P, LC, 36])
    raw = sb(ctx, "raw", [P, 2, D])
    front = ExitStack()
    cmask = sb(front, "cmask", [P, P], BF16)
    ident_b = sb(front, "ident_b", [P, P], BF16)
    smask = sb(front, "smask", [P, 2, P], BF16)
    e_head = sb(front, "e_head", [72, H, P], BF16)
    e_row = sb(front, "e_row", [P, PAIRS * 2, P], BF16)
    c_prompt = sb(front, "c_prompt", [72, SEQ], BF16)
    c_past = sb(front, "c_past", [P, 2, KEYS], BF16)
    kgain = sb(front, "kgain", [P, DH])
    qgain = sb(front, "qgain", [P, 1])

    NL = NT * H + LC
    lru = ExitStack()
    wl_hi = sb(lru, "wl_hi", [P, 2, KC, P], F32R)
    wl_lo = sb(lru, "wl_lo", [P, 2, KC, P], F32R)
    f_rows = sb(lru, "f_rows", [H, T_ALL])
    l_in = sb(lru, "l_in", [P, NL])
    l_e = sb(lru, "l_e", [P, NL])
    l_s = sb(lru, "l_s", [P, NL])
    l_q = sb(lru, "l_q", [P, NL])
    cl = sb(lru, "cl", [P, KP, DEC_B * H])
    lf_own = sb(lru, "lf_own", [P, DEC_B, H])
    ones_w = sb(lru, "ones_w", [64, 512])
    cc = sb(lru, "cc", [64, KEYS])
    cc_new = sb(lru, "cc_new", [64, DEC_T])
    c_new = sb(lru, "c_new", [64, DEC_T])
    c_mid = sb(lru, "c_mid", [64, KEYS], BF16)
    cp = sb(lru, "cp", [H, SEQ])
    cp_mid = sb(lru, "cp_mid", [H, SEQ], BF16)
    block_of = sb(lru, "block_of", [P, DEC_B])
    xpad = sb(lru, "xpad", [P, 3 + SEQ])
    spad = sb(lru, "spad", [P, DEC_B, 3 + DEC_T])
    pc = sb(lru, "pc", [P, PW])
    gate_w = sb(lru, "gate_w", [P, 2, P])
    l_f = sb(lru, "l_f", [P, NL])
    start = ExitStack()
    x_in = sb(start, "x_in", [P, 3, D])
    ln1_b = sb(start, "ln1_b", [P, D])
    rows = sb(start, "rows", [ROWS, LW])
    wf_raw = sb(start, "wf_raw", [P, KC, H])
    wf_hi = sb(start, "wf_hi", [P, KC, H], F32R)
    wf_lo = sb(start, "wf_lo", [P, KC, H], F32R)
    bf_b = sb(start, "bf_b", [P, H])
    build = sb(start, "build", [P, H * P])
    build2 = sb(start, "build2", [P, P])
    start.close()
    work = ExitStack()
    xc = sb(work, "xc", [P, T_ALL])
    gy = sb(work, "gy", [P, T_ALL])
    tr = sb(work, "tr", [P, T_ALL])
    decay = sb(work, "decay", [P, T_ALL])
    a2 = sb(work, "a2", [P, T_ALL])
    tl = sb(work, "tl", [P, T_ALL])
    ti = sb(work, "ti", [P, T_ALL])
    ah = sb(work, "ah", [P, DEC_B])
    work.close()
    lru.close()
    pair = ExitStack()
    PW3 = 3 * P
    wp_hi = sb(pair, "wp_hi", [P, KC, PW3], F32R)
    wp_lo = sb(pair, "wp_lo", [P, KC, PW3], F32R)
    qt = sb(pair, "qt", [P, T_ALL])
    kt_all = sb(pair, "kt_all", [P, T_ALL])
    vt = sb(pair, "vt", [P, NT, P])
    qk = sb(pair, "qk", [P, 3, 2 * P])
    sqj = sb(pair, "sqj", [P, 2 * P])
    s4 = sb(pair, "s4", [P, 2, 4])
    m4 = sb(pair, "m4", [P, 2, 4])
    rs4 = sb(pair, "rs4", [P, 2, 4])
    probs = sb(pair, "probs", [P, 2, D])
    pts = sb(pair, "pts", [P, 8, 512])
    k_c = sb(pair, "k_c", [P, 2, KP, P])
    v_c = sb(pair, "v_c", [P, 4, KP, P])
    q_blocks = sb(pair, "q_blocks", [P, DEC_B, 2, DEC_T])
    top = sb(pair, "top", [P, 2])
    neg_top = sb(pair, "neg_top", [P, 2])
    den = sb(pair, "den", [P, 2])
    rden = sb(pair, "rden", [P, 2])
    pair.close()
    front.close()
    out = ExitStack()
    wo_hi = sb(out, "wo_hi", [P, KC, D], F32R)
    wo_lo = sb(out, "wo_lo", [P, KC, D], F32R)
    x_e = sb(out, "x_e", [P, 2, KC, P])
    sq = sb(out, "sq", [P, KC, P])
    ssq = sb(out, "ssq", [P, 2, P])
    ln2_b = sb(out, "ln2_b", [P, KC, P])
    ms2 = sb(out, "ms2", [P, 2, 2])
    rs2 = sb(out, "rs2", [P, 2, 2])
    kept = sb(out, "kept", [36, LW])
    out.close()
    mlp = ExitStack()
    u_hi = sb(mlp, "u_hi", [P, 2, 2, T_ALL], F32R)
    u_lo = sb(mlp, "u_lo", [P, 2, 2, T_ALL], F32R)
    wu_hi = sb(mlp, "wu_hi", [P, 2, KC, P], F32R)
    wu_lo = sb(mlp, "wu_lo", [P, 2, KC, P], F32R)
    wd_hi = sb(mlp, "wd_hi", [P, 2, D], F32R)
    wd_lo = sb(mlp, "wd_lo", [P, 2, D], F32R)
    up = sb(mlp, "up", [P, G, GN])
    mlp.close()
    psum = ctx.enter_context(nc.psum_tensor("psum", [P, 8, 512], F32))

    x_landed = [sem(f"x_landed{i}") for i in range(3)]
    small_in = sem("small_in")
    wf_in = sem("wf_in")
    consts_built = sem("consts_built")
    consts_ready = sem("consts_ready")
    x_squared = sem("x_squared")
    x_mean = sem("x_mean")
    x_rstd = sem("x_rstd")
    x_normed = sem("x_normed")
    x_turned = sem("x_turned")
    h_hi_ready = sem("h_hi_ready")
    h_lo_ready = sem("h_lo_ready")
    rows_turned = sem("rows_turned")
    wf_split = sem("wf_split")
    f_done = sem("f_done")
    f_copied = sem("f_copied")
    f_turned = sem("f_turned")
    wf_ready = sem("wf_ready")
    params_copied = sem("params_copied")
    c_read = sem("c_read")
    pair_proj, pair_sq, v_done = sem("pair_proj"), sem("pair_sq"), sem("v_done")
    s4_ready, rs4_ready, qk_ready, qk_turned = sem("s4_ready"), sem("rs4_ready"), sem("qk_ready"), sem("qk_turned")
    q_done, k_done = sem("q_done"), sem("k_done")
    k_out = [sem(f"k_out{i}") for i in range(3)]
    v_out = sem("v_out")
    scores, top_ready, exp_done, probs_ready = sem("scores"), sem("top_ready"), sem("exp_done"), sem("probs_ready")
    p_turned, pt_a, pt_b, pv_done, o_done = sem("p_turned"), sem("pt_a"), sem("pt_b"), sem("pv_done"), sem("o_done")
    q_blocks_ready = sem("q_blocks_ready")
    kc_in = [sem(f"kc_in{i}") for i in range(2)]
    vc_in = [sem(f"vc_in{i}") for i in range(4)]
    kc_turned, kts_a, kts_b = sem("kc_turned"), sem("kts_a"), sem("kts_b")
    s_scores, s_top, s_exp, s_probs = sem("s_scores"), sem("s_top"), sem("s_exp"), sem("s_probs")
    s_turned, s_pta, s_ptb, s_pv, s_out = sem("s_turned"), sem("s_pta"), sem("s_ptb"), sem("s_pv"), sem("s_out")
    ln2_in, keep_in = sem("ln2_in"), sem("keep_in")
    xe_in = [sem("xe_in0"), sem("xe_in1")]
    mix_sq, mix_ssq, mix_sums, mix_ms, mix_rs = sem("mix_sq"), sem("mix_ssq"), sem("mix_sums"), sem("mix_ms"), sem("mix_rs")
    mix_hi, mix_lo, out_done = sem("mix_hi"), sem("mix_lo"), sem("out_done")
    x1_ready, x1_sq, x1_ms, x1_rs = sem("x1_ready"), sem("x1_sq"), sem("x1_ms"), sem("x1_rs")
    h2_ready, h2_turned, h2_hi, h2_lo = sem("h2_ready"), sem("h2_turned"), sem("h2_hi"), sem("h2_lo")
    up_done, up_read, up_squared, u_ready = sem("up_done"), sem("up_read"), sem("up_squared"), sem("u_ready")
    down_done, y_added = sem("down_done"), sem("y_added")
    SMALL = 1 + 1 + 6 + 1 + 1 + 1 + 1 + 2 + KP
    l_abs = sem("l_abs")
    l_exp = sem("l_exp")
    logf_ready = sem("logf_ready")
    gates_free = sem("gates_free")
    raw_in = [sem("raw_in0"), sem("raw_in1")]
    w_hi = sem("w_hi")
    w_lo = sem("w_lo")
    proj_done = sem("proj_done")
    gate_done = sem("gate_done")
    gw_in = sem("gw_in")
    xr_copied = sem("xr_copied")
    gate_read = sem("gate_read")
    decays_ready = sem("decays_ready")
    xc_ready = sem("xc_ready")
    one_minus_a2 = sem("one_minus_a2")
    root_ready = sem("root_ready")
    mix_ready = sem("mix_ready")
    dve_step = sem("dve_step")
    act_step = sem("act_step")
    pool_step = sem("pool_step")
    stored = sem("stored")
    kept_turned = sem("kept_turned")
    kept_copied = sem("kept_copied")
    c_turned = sem("c_turned")
    c_own_ready = sem("c_own_ready")
    c_ready = sem("c_ready")

    def flat(ap):
        return ap.rearrange("a b d -> (a b) d")

    xp_rows = flat(x_prompt)
    xs_rows = flat(x_sample)

    def x_rows(t):
        return xp_rows[t * P:(t + 1) * P, :] if t < SEQ // P else xs_rows[:, :]

    w_in_k = w_in[0].rearrange("(k p) n -> p k n", p=P)
    V_OUT = 2 * LC + 4 * PAIRS
    V_MLP = V_OUT + KC
    RAW_OUT = 64 + 64 * PAIRS
    RAW_MLP = RAW_OUT + 64
    MLP_STEPS = NFB - 1

    def up_bank(par, m):
        return (6 * par + m) % 4

    def mlp_raw(q):
        return RAW_MLP + 16 * (q + 1)

    DVE_PAIR = 54
    PB = [0, 1, 4]
    QB, KB = [2, 6, 2], [3, 7, 3]
    SB = [4, 6]
    SPAN = 4 * P

    def step_of(s):
        return s // 8, (s // 4) % 2, s % 4

    def two_banks(b):
        return psum[:, b:b + 2, :].rearrange("p a n -> p (a n)")

    DVE_LRU = 16
    ACT_LRU = 2

    class Steps:

        def __init__(self, eng, s):
            self.eng, self.s, self.n, self.base = eng, s, 0, 0

        def did(self, ins):
            ins.then_inc(self.s, 1)
            self.n += 1

        def link(self, ins):
            self.did(ins)
            self.eng.wait_ge(self.s, self.base + self.n)

        def enter(self, i, per, before):
            self.base, self.n = before + i * per, 0

        def leave(self, per, before, times):
            assert self.n == per, (self.n, per)
            self.base, self.n = 0, before + per * times

    with nc.allow_non_contiguous_dma(reason="narrow columns of small arrays"), nc.Block() as block:

        @block.sync
        def _(sp):
            n_stored = 0

            def store(dst, src):
                nonlocal n_stored
                sp.dma_start(dst, src).then_inc(stored, 16)
                n_stored += 1

            sp.dma_start(x_in[:, 0, :], x_rows(0)).then_inc(x_landed[0], 16)
            sp.dma_start(ln1_b[:], ln1.to_broadcast([P, D])).then_inc(small_in, 16)
            sp.dma_start(x_in[:, 1, :], x_rows(1)).then_inc(x_landed[1], 16)
            sp.dma_start(x_in[:, 2, :], x_rows(2)).then_inc(x_landed[2], 16)
            sp.dma_start(rows[R_CONVW:R_CONVW + CW, :], conv_w[0]).then_inc(small_in, 16)
            for r, a in ((R_CONVB, conv_b), (R_BGA, b_gate_a), (R_BGX, b_gate_x), (R_LAM, lru_lambda),
                         (R_GAO, g_attn_out), (R_GLO, g_lru_out)):
                sp.dma_start(rows[r:r + 1, :], a).then_inc(small_in, 16)
            sp.dma_start(rows[R_H0:R_H0 + DEC_B, :], state_h[0]).then_inc(small_in, 16)
            sp.dma_start(rows[R_CONV:ROWS, :], state_conv[0].rearrange("b j c -> (b j) c")).then_inc(small_in, 16)
            sp.dma_start(bf_b[:], b_f.to_broadcast([P, H])).then_inc(small_in, 16)
            sp.dma_start(kgain[:], k_gain.to_broadcast([P, DH])).then_inc(small_in, 16)
            for hp in range(2):
                sp.dma_start(qgain[hp * DH:(hp + 1) * DH, :], q_gain.rearrange("a d -> d a")).then_inc(small_in, 16)
            sp.dma_start(wf_raw[:], w_in_k[:, :, F_COL:F_COL + H]).then_inc(wf_in, 16)
            for kt in range(KP):
                sp.dma_start(cl[:, kt, :].rearrange("p (b h) -> p b h", b=DEC_B),
                             cache_logf[0, :, kt * P:(kt + 1) * P, :].rearrange("b p h -> p b h")).then_inc(small_in, 16)
            for t in range(3, NT):
                sp.wait_ge(x_turned, 2 * (t - 3) + 2)
                sp.dma_start(x_in[:, t % 3, :], x_rows(t)).then_inc(x_landed[t % 3], 16)

            def lru_weights(c, u):
                sp.dma_start(raw[:, u, :].rearrange("p (k n) -> p k n", k=KC),
                             w_in_k[:, :, bass.ds((XR_COL, YG_COL)[u] + c * P, P)]).then_inc(raw_in[u], 16)

            def gates(c):
                for g, w in enumerate((w_gate_a, w_gate_x)):
                    for b in range(2):
                        sp.dma_start(gate_w[b * DH:(b + 1) * DH, g, b * DH:(b + 1) * DH],
                                     w[0, bass.ds(2 * c + b, 1), :, :].rearrange("a i j -> (a i) j")).then_inc(gw_in, 16)

            lru_weights(0, 0)
            lru_weights(0, 1)
            sp.wait_ge(gates_free, 1)
            gates(0)
            with sp.Fori(0, LC - 1) as c:
                sp.wait_ge(w_lo, 2 * c + 1)
                lru_weights(c + 1, 0)
                sp.wait_ge(w_lo, 2 * c + 2)
                lru_weights(c + 1, 1)
                sp.wait_ge(gate_done, 6 * c + 6)
                gates(c + 1)
            sp.wait_ge(logf_ready, 1)
            for t in range(NT - 1):
                store(logf_prompt[0, 0, t * P:(t + 1) * P, :], l_f[:, t * H:(t + 1) * H])
            store(logf_sample[0].rearrange("b t h -> (b t) h"), l_f[:, (NT - 1) * H:NT * H])
            def pair_weights(p, j):
                for kk in range(2):
                    sp.dma_start(raw[:, j % 2, kk * PW3:(kk + 1) * PW3].rearrange("p (a n) -> p a n", a=3),
                                 w_in[0, (2 * j + kk) * P:(2 * j + kk + 1) * P, 0:3 * AW].rearrange(
                                     "p (a n) -> p a n", a=3)[:, :, bass.ds(p * P, P)]).then_inc(raw_in[j % 2], 16)

            def past_keys(p, b):
                sp.dma_start(k_c[:, b % 2, :, :], cache_k[0, b, :, bass.ds(2 * p, 2), :].rearrange(
                    "(t p) h d -> p t (h d)", p=P)).then_inc(kc_in[b % 2], 16)

            def past_values(p, b):
                sp.dma_start(v_c[:, b % 4, :, :], cache_v[0, b, :, bass.ds(2 * p, 2), :].rearrange(
                    "(t p) h d -> p t (h d)", p=P)).then_inc(vc_in[b % 4], 16)

            for j in range(4):
                sp.wait_ge(w_lo, 7 + j)
                pair_weights(0, j)
            sp.wait_ge(mix_ready, LC + 1)
            sp.wait_ge(stored, 16 * n_stored)
            for b in range(4):
                past_values(0, b)
            for b in range(2):
                past_keys(0, b)

            def pair_transfers(p, last):
                for t in range(NT):
                    sp.wait_ge(qk_ready, NT * p + t + 1)
                    rows_of = k_prompt[0, 0, t * P:(t + 1) * P] if t < NT - 1 else k_sample[0].rearrange("b t h d -> (b t) h d")
                    sp.dma_start(rows_of[:, bass.ds(2 * p, 2), :],
                                 qk[:, t % 3, P:2 * P].rearrange("p (h d) -> p h d", h=2)).then_inc(k_out[t % 3], 16)
                sp.wait_ge(v_done, NT * p + NT)
                sp.dma_start(v_prompt[0, 0].rearrange("(t p) h d -> p t h d", p=P)[:, :, bass.ds(2 * p, 2), :].rearrange(
                    "p t h d -> p t (h d)"), vt[:, 0:NT - 1, :]).then_inc(v_out, 16)
                sp.dma_start(v_sample[0].rearrange("b t h d -> (b t) h d")[:, bass.ds(2 * p, 2), :],
                             vt[:, NT - 1, :].rearrange("p (h d) -> p h d", h=2)).then_inc(v_out, 16)
                for i in range(3):
                    sp.wait_ge(k_out[i], 48 * p + 48)
                sp.wait_ge(v_out, 32 * p + 32)
                if not last:
                    for j in range(4):
                        sp.wait_ge(w_lo, 4 * p + 11 + j)
                        pair_weights(p + 1, j)
                for b in range(2, DEC_B):
                    sp.wait_ge(kc_turned, DEC_B * p + b - 1)
                    past_keys(p, b)
                sp.wait_ge(s_pv, 2 * p + 1)
                for b in range(4, DEC_B):
                    past_values(p, b)
                if not last:
                    sp.wait_ge(s_pv, 2 * p + 2)
                    for b in range(4):
                        past_values(p + 1, b)
                    for b in range(2):
                        past_keys(p + 1, b)

            with sp.Fori(0, PAIRS - 1) as p:
                pair_transfers(p, False)
            pair_transfers(PAIRS - 1, True)
            for j in range(KC):
                sp.wait_ge(w_lo, V_OUT + j - 1)
                sp.dma_start(raw[:, j % 2, :], w_out[0, j * P:(j + 1) * P, :]).then_inc(raw_in[j % 2], 16)
            sp.wait_ge(s_out, PAIRS + 1)
            sp.dma_start(ln2_b[:].rearrange("p k n -> p (k n)"), ln2.to_broadcast([P, D])).then_inc(ln2_in, 16)

            def load_xe(t):
                sp.dma_start(x_e[:, t % 2, :, :].rearrange("p k n -> p (k n)"), x_rows(t)).then_inc(xe_in[t % 2], 16)

            def up_weights(b, c, slot_free):
                sp.wait_ge(w_lo, slot_free)
                sp.dma_start(raw[:, c, :].rearrange("p (k n) -> p k n", k=KC),
                             w_up[0].rearrange("(k p) n -> p k n", p=P)[:, :, bass.ds(b * FB + c * P, P)]
                             ).then_inc(raw_in[c], 16)

            def down_weights(i, k, slot_free):
                sp.wait_ge(w_lo, slot_free)
                sp.dma_start(raw[:, k, :], w_down[0, bass.ds(i * FB + k * P, P), :]).then_inc(raw_in[k], 16)

            load_xe(0)
            load_xe(1)
            for c in range(2):
                up_weights(0, c, V_MLP + c - 1)
            sp.wait_ge(kept_copied, 1)
            store(h_prompt[0, :, :], kept[0:1, :])
            store(h_sample[0, :, :], kept[1:9, :])
            store(conv_prompt[0, 0, :, :], kept[9:12, :])
            store(conv_sample[0].rearrange("b j c -> (b j) c"), kept[12:36, :])
            for t in range(2, NT):
                sp.wait_ge(h2_turned, 2 * (t - 2) + 2)
                load_xe(t)
            sp.wait_ge(stored, 16 * n_stored)
            for c in range(2):
                up_weights(1, c, V_MLP + 2 + c - 1)
            with sp.Fori(0, MLP_STEPS - 1) as i:
                for k in range(2):
                    down_weights(i, k, V_MLP + 4 * i + 4 + k - 1)
                for c in range(2):
                    up_weights(i + 2, c, V_MLP + 4 * i + 6 + c - 1)
            for k in range(2):
                down_weights(MLP_STEPS - 1, k, V_MLP + 4 * MLP_STEPS + k - 1)
            for k in range(2):
                down_weights(NFB - 1, k, V_MLP + 4 * MLP_STEPS + 2 + k - 1)
            for t in range(NT):
                sp.wait_ge(y_added, 4 + 2 * NT * (NFB - 1) + 2 * t + 2)
                rows_of = y_prompt[0, t * P:(t + 1) * P, :] if t < NT - 1 else y_sample.rearrange("b t d -> (b t) d")
                store(rows_of.rearrange("p (k n) -> p k n", k=KC), mix[:, :, t * P:(t + 1) * P])
            sp.wait_ge(stored, 16 * n_stored)

        @block.gpsimd
        def _(pool):
            n = Steps(pool, consts_built)
            n.link(nc.gpsimd.memset(ident[:], 0.0))
            n.link(nc.gpsimd.affine_select(ident[:], ident[:], [[-1, P]], ALU.not_equal, 1.0, base=0, channel_multiplier=1))
            n.link(nc.gpsimd.memset(neg_half[:], -0.5))
            nc.gpsimd.memset(ones_col[:], 1.0).then_inc(consts_ready, 1)
            for t in range(NT):
                pool.wait_ge(x_mean, t + 1)
                nc.gpsimd.tensor_tensor(x_rs[:, t:t + 1], x_ms[:, t:t + 1], neg_half[:, 0:1], ALU.pow).then_inc(x_rstd, 1)
            nc.gpsimd.memset(gate_w[:], 0.0).then_inc(gates_free, 1)
            n.link(nc.gpsimd.memset(ones_w[:], 1.0))
            n.link(nc.gpsimd.memset(c_prompt[:], 0.0))
            n.link(nc.gpsimd.memset(c_past[:], 0.0))
            n.link(nc.gpsimd.memset(build2[:], 0.0))
            n.link(nc.gpsimd.affine_select(build2[:], build2[:], [[-1, P]], ALU.is_ge, MASKED, base=0, channel_multiplier=1))
            n.link(nc.gpsimd.tensor_copy(cmask[:], build2[:]))
            n.link(nc.gpsimd.tensor_copy(ident_b[:], ident[:]))
            n.link(nc.gpsimd.memset(block_of[:], 1.0))
            n.link(nc.gpsimd.affine_select(block_of[:], block_of[:], [[-DEC_T, DEC_B]], ALU.is_ge, 0.0, base=0,
                                           channel_multiplier=1))
            n.link(nc.gpsimd.affine_select(block_of[:], block_of[:], [[DEC_T, DEC_B]], ALU.is_ge, 0.0,
                                           base=DEC_T - 1, channel_multiplier=-1))
            eh = build[:, :].rearrange("p (h m) -> p h m", h=H)
            n.link(nc.gpsimd.memset(build[:], 0.0))
            for r in range(3):
                n.link(nc.gpsimd.affine_select(eh, eh, [[-1, H], [0, P]], ALU.not_equal, 1.0, base=-32 * r,
                                               channel_multiplier=1))
            n.link(nc.gpsimd.tensor_copy(e_head[:], eh[0:72]))
            er = build[:, :].rearrange("p (a g h q) -> p a g h q", a=PAIRS, g=DEC_B, h=2)
            n.link(nc.gpsimd.memset(build[:], 0.0))
            for r in range(2):
                n.link(nc.gpsimd.affine_select(er, er, [[-2, PAIRS], [-8, DEC_B], [-1, 2], [0, DEC_T]], ALU.not_equal,
                                               1.0, base=-64 * r, channel_multiplier=1))
            n.link(nc.gpsimd.tensor_copy(e_row[:].rearrange("p a m -> p (a m)"), build[:]))
            for g in range(2):
                for hp, fill in enumerate((-(2.0 ** 50), 2.0 ** 50)):
                    v = build[:, hp * P:(hp + 1) * P].rearrange("p (b t) -> p b t", b=DEC_B)
                    n.link(nc.gpsimd.memset(build[:, hp * P:(hp + 1) * P], 0.0))
                    n.link(nc.gpsimd.affine_select(v, v, [[-32, DEC_B], [-1, DEC_T]], ALU.is_ge, fill,
                                                   base=P * g - DEC_T * hp, channel_multiplier=1))
                    n.link(nc.gpsimd.affine_select(v, v, [[32, DEC_B], [0, DEC_T]], ALU.is_ge, fill,
                                                   base=DEC_T * (hp + 1) - 1 - P * g, channel_multiplier=-1))
                n.link(nc.gpsimd.tensor_tensor(build[:, 0:P], build[:, 0:P], build[:, P:2 * P], ALU.mult))
                n.link(nc.gpsimd.tensor_copy(smask[:, g, :], build[:, 0:P]))
            nc.gpsimd.memset(xpad[:, 0:3], 0.0).then_inc(consts_ready, 1)
            def pair_rstd(p):
                for t in range(NT):
                    pool.wait_ge(s4_ready, NT * p + t + 1)
                    nc.gpsimd.tensor_tensor(rs4[:, t % 2, :], m4[:, t % 2, :], neg_half[:], ALU.pow).then_inc(rs4_ready, 1)

            with pool.Fori(0, PAIRS) as p:
                pair_rstd(p)
            def mix_rstd(t):
                pool.wait_ge(mix_ms, t + 1)
                nc.gpsimd.tensor_tensor(rs2[:, t % 2, :], ms2[:, t % 2, :], neg_half[:, 0:2], ALU.pow).then_inc(mix_rs, 1)

            mix_rstd(0)
            for t in range(NT):
                if t < NT - 1:
                    mix_rstd(t + 1)
                pool.wait_ge(x1_ms, t + 1)
                nc.gpsimd.tensor_tensor(x_rs[:, t:t + 1], x_ms[:, t:t + 1], neg_half[:, 0:1], ALU.pow).then_inc(x1_rs, 1)

        @block.scalar
        def _(act):
            a = Steps(act, act_step)

            def turn_hi(t):
                for b in range(2):
                    act.wait_ge(x_turned, 2 * t + b + 1)
                    nc.scalar.copy(h_hi[:, 4 * b:4 * b + 4, t * P:(t + 1) * P],
                                   psum[:, 2 * (t % 2) + b, :].rearrange("p (k n) -> p k n", k=4)).then_inc(h_hi_ready, 1)

            for t in range(NT):
                act.wait_ge(x_landed[t % 3], 16 * (t // 3 + 1))
                if t >= 1:
                    act.wait_ge(x_squared, t)
                nc.scalar.activation(mix[:, 0, 0:D], x_in[:, t % 3, :], ACT.Square,
                                     accum_out=x_ss[:, t:t + 1]).then_inc(x_squared, 1)
                if t >= 1:
                    turn_hi(t - 1)
            turn_hi(NT - 1)
            act.wait_ge(wf_in, 16)
            nc.scalar.copy(wf_hi[:], wf_raw[:]).then_inc(wf_split, 1)

            def lru_hi(c, u):
                act.wait_ge(raw_in[u], 16 * c + 16)
                nc.scalar.copy(wl_hi[:, u, :, :].rearrange("p k n -> p (k n)"), raw[:, u, :]).then_inc(w_hi, 1)

            lru_hi(0, 0)
            lru_hi(0, 1)
            for g in range(G):
                act.wait_ge(f_done, g + 1)
                nc.scalar.copy(f_rows[:, g * GN:(g + 1) * GN], psum[0:H, 5 + g, 0:GN]).then_inc(f_copied, 1)
            act.wait_ge(l_abs, 1)
            nc.scalar.activation(l_e[:], l_e[:], ACT.Exp, scale=-1.0).then_inc(l_exp, 1)

            def chunk(c, last):
                for g in range(G):
                    act.wait_ge(proj_done, 6 * c + g + 1)
                    if g < 2:
                        nc.scalar.copy(xpad[:, 3 + g * GN:3 + (g + 1) * GN], psum[:, g, 0:GN]).then_inc(xr_copied, 1)
                nc.scalar.copy(xpad[:, 3 + 2 * GN:], psum[:, 2, 0:SEQ - 2 * GN]).then_inc(xr_copied, 1)
                nc.scalar.copy(spad[:, :, 3:], psum[:, 2, SEQ - 2 * GN:GN].rearrange(
                    "p (b t) -> p b t", b=DEC_B)).then_inc(xr_copied, 1)
                if not last:
                    lru_hi(c + 1, 0)
                act.wait_ge(mix_ready, c + 1)
                for g in range(G):
                    act.wait_ge(proj_done, 6 * c + 3 + g + 1)
                    nc.scalar.activation(gy[:, g * GN:(g + 1) * GN], psum[:, 3 + g, 0:GN], ACT.Gelu_apprx_tanh)
                if not last:
                    lru_hi(c + 1, 1)
                for m in range(6):
                    act.wait_ge(gate_done, 6 * c + m + 1)
                    dst, g = (tr, ti)[m // 3], m % 3
                    nc.scalar.activation(dst[:, g * GN:(g + 1) * GN], psum[:, 6 + m % 2, 0:GN], ACT.Tanh, scale=0.5,
                                         bias=pc[:, R_HBGA + m // 3:R_HBGA + m // 3 + 1]).then_inc(gate_read, 1)
                act.wait_ge(gate_read, 6 * c + 6)
                a.link(nc.scalar.activation(decay[:], tr[:], ACT.Exp, scale=pc[:, R_NSP4:R_NSP4 + 1],
                                            bias=pc[:, R_NSP4:R_NSP4 + 1]))
                a.did(nc.scalar.activation(tl[:], tr[:], ACT.Tanh, scale=pc[:, R_SP4:R_SP4 + 1],
                                           bias=pc[:, R_SP4:R_SP4 + 1]))
                nc.scalar.activation(a2[:], decay[:], ACT.Square).then_inc(decays_ready, 1)
                act.wait_ge(one_minus_a2, c + 1)
                nc.scalar.activation(tr[:], a2[:], ACT.Sqrt, scale=0.25).then_inc(root_ready, 1)

            act.wait_ge(consts_ready, 2)
            before = a.n
            with act.Fori(0, LC - 1) as c:
                a.enter(c, ACT_LRU, before)
                chunk(c, False)
                a.leave(ACT_LRU, before, LC - 1)
            a.enter(LC - 1, ACT_LRU, before)
            chunk(LC - 1, True)
            a.leave(ACT_LRU, before, LC)
            def pair_hi(p, j):
                act.wait_ge(raw_in[j % 2], 64 + 64 * p + 32 * (j // 2) + 32)
                nc.scalar.copy(wp_hi[:, 2 * j:2 * j + 2, :].rearrange("p k n -> p (k n)"),
                               raw[:, j % 2, 0:2 * PW3]).then_inc(w_hi, 1)

            act.wait_ge(c_ready, 1)
            act.wait_ge(proj_done, 6 * LC)
            for j in range(4):
                pair_hi(0, j)
            act.wait_ge(mix_ready, LC + 1)
            nc.scalar.copy(den[:], ident[:, 0:2]).then_inc(s_out, 1)

            def pair_act(p, last):
                def q_out(g):
                    n = SPAN if g < 2 else P
                    act.wait_ge(qk_turned, NT * p + min(4 * g + 4, NT))
                    nc.scalar.activation(qt[:, g * SPAN:g * SPAN + n], psum[:, QB[g], 0:n], ACT.Copy,
                                         scale=qgain[:, 0:1]).then_inc(q_done, 1)

                for t in range(NT):
                    act.wait_ge(pair_proj, NT * p + t + 1)
                    nc.scalar.copy(vt[:, t, :], psum[:, PB[t % 3], 2 * P:PW3]).then_inc(v_done, 1)
                    if t >= 1:
                        act.wait_ge(s4_ready, NT * p + t)
                    nc.scalar.activation(sqj[:], psum[:, PB[t % 3], 0:2 * P], ACT.Square).then_inc(pair_sq, 1)
                    if t == 6:
                        q_out(0)
                q_out(1)
                q_out(2)

                def exp(s):
                    nk = 4 * step_of(s)[1] + step_of(s)[2] + 1
                    act.wait_ge(top_ready, 16 * p + s + 1)
                    nc.scalar.activation(probs[:, s % 2, 0:nk * P], two_banks(SB[s % 2])[:, 0:nk * P], ACT.Exp,
                                         bias=neg_top[:, s % 2:s % 2 + 1],
                                         accum_out=den[:, s % 2:s % 2 + 1]).then_inc(exp_done, 1)

                def turned_a(s):
                    _, g, j = step_of(s)
                    n = min(4 * g + j + 1, 4)
                    act.wait_ge(p_turned, 16 * p + s + 1)
                    nc.scalar.copy(pts[:, 0:n, j * P:(j + 1) * P],
                                   psum[:, 2, 0:n * P].rearrange("p (k n) -> p k n", n=P)).then_inc(pt_a, 1)

                def heads_out(gi):
                    hp, g = gi // 2, gi % 2
                    act.wait_ge(pv_done, 4 * p + gi + 1)
                    nc.scalar.copy(mix[hp * DH:(hp + 1) * DH, bass.ds(p, 1), g * SPAN:(g + 1) * SPAN].rearrange(
                        "p a n -> p (a n)"), psum[hp * DH:(hp + 1) * DH, gi % 2, :]).then_inc(o_done, 1)

                exp(0)
                for s in range(16):
                    if s >= 1:
                        turned_a(s - 1)
                    if s < 15:
                        exp(s + 1)
                    if s % 4 == 1 and s > 1:
                        heads_out(s // 4 - 1)
                    if not last and s in (3, 5, 7, 9):
                        pair_hi(p + 1, (s - 3) // 2)
                turned_a(15)
                heads_out(3)
                for b in range(0, DEC_B, 2):
                    act.wait_ge(kc_turned, DEC_B * p + b + 1)
                    nc.scalar.copy(pts[:, 2, :], psum[:, 2, :]).then_inc(kts_a, 1)
                for g in range(2):
                    act.wait_ge(s_top, 2 * p + g + 1)
                    nc.scalar.activation(probs[:, g, 0:KEYS], two_banks(SB[g])[:, 0:KEYS], ACT.Exp,
                                         bias=neg_top[:, g:g + 1], accum_out=den[:, g:g + 1]).then_inc(s_exp, 1)
                for g in range(2):
                    act.wait_ge(s_turned, 2 * p + g + 1)
                    nc.scalar.copy(pts[:, 0, :], psum[:, 2, :]).then_inc(s_pta, 1)
                    act.wait_ge(s_pv, 2 * p + g + 1)
                    for hp in range(2):
                        last_out = nc.scalar.copy(
                            mix[hp * DH:(hp + 1) * DH, bass.ds(p, 1), SEQ + g * DH:SEQ + (g + 1) * DH].rearrange(
                                "p a (b q) -> p (a b) q", b=4),
                            psum[hp * DH:(hp + 1) * DH, g, 0:P].rearrange("p (b h q) -> p b h q", b=4, h=2)[:, :, hp, :])
                last_out.then_inc(s_out, 1)

            with act.Fori(0, PAIRS - 1) as p:
                pair_act(p, False)
            pair_act(PAIRS - 1, True)
            def tile(t):
                return slice(t * P, (t + 1) * P)

            act.wait_ge(s_pv, 2 * PAIRS)
            for j in range(KC):
                r = R_GAO if j < LC else R_GLO
                act.wait_ge(raw_in[j % 2], RAW_OUT + 16 * (j // 2) + 16)
                nc.scalar.activation(wo_hi[:, j, :], raw[:, j % 2, :], ACT.Copy,
                                     scale=param[:, j % LC, r:r + 1]).then_inc(w_hi, 1)
                if j == 1:
                    act.wait_ge(s_out, PAIRS + 1)
                    nc.scalar.activation(sq[:], mix[:, :, tile(0)], ACT.Square).then_inc(mix_sq, 1)
                    nc.scalar.copy(h_hi[:, :, tile(0)], mix[:, :, tile(0)]).then_inc(mix_hi, 1)
            act.wait_ge(kept_turned, 1)
            nc.scalar.copy(kept[:], psum[0:36, 7, :]).then_inc(kept_copied, 1)

            def up_hi(b, c, landed, freed):
                act.wait_ge(raw_in[c], landed)
                act.wait_ge(up_done, freed)
                nc.scalar.copy(wu_hi[:, c, :, :].rearrange("p k n -> p (k n)"), raw[:, c, :]).then_inc(w_hi, 1)

            for t in range(NT):
                if t < NT - 1:
                    act.wait_ge(mix_ssq, t + 1)
                    nc.scalar.activation(sq[:], mix[:, :, tile(t + 1)], ACT.Square).then_inc(mix_sq, 1)
                    nc.scalar.copy(h_hi[:, :, tile(t + 1)], mix[:, :, tile(t + 1)]).then_inc(mix_hi, 1)
                else:
                    act.wait_ge(out_done, 2 * NT)
                    for c in range(2):
                        act.wait_ge(raw_in[c], RAW_MLP + 16)
                        nc.scalar.copy(wu_hi[:, c, :, :].rearrange("p k n -> p (k n)"), raw[:, c, :]).then_inc(w_hi, 1)
                act.wait_ge(x1_ready, t + 1)
                nc.scalar.activation(x_e[:, t % 2, :, :], mix[:, :, tile(t)], ACT.Square,
                                     accum_out=x_ss[:, t:t + 1]).then_inc(x1_sq, 1)
                for u in ([t - 1] if t < NT - 1 else [t - 1, t]) if t else []:
                    for b in range(2):
                        act.wait_ge(h2_turned, 2 * u + b + 1)
                        nc.scalar.copy(h_hi[:, 4 * b:4 * b + 4, tile(u)],
                                       psum[:, 4 + b, :].rearrange("p (k n) -> p k n", k=4)).then_inc(h2_hi, 1)

            def relu_squared(b, par, m, first=False):
                n = 6 * b + m
                act.wait_ge(up_done, n + 1)
                if m >= 3:
                    act.wait_ge(u_ready, n - 2)
                elif not first:
                    act.wait_ge(u_ready, 6 * b)
                nc.scalar.activation(up[:, m % 3, :], psum[:, up_bank(par, m), 0:GN], ACT.Relu).then_inc(up_read, 1)
                act.wait_ge(up_read, n + 1)
                nc.scalar.activation(up[:, m % 3, :], up[:, m % 3, :], ACT.Square).then_inc(up_squared, 1)

            def down_hi(i, k, landed):
                act.wait_ge(raw_in[k], landed)
                nc.scalar.copy(wd_hi[:, k, :], raw[:, k, :]).then_inc(w_hi, 1)

            for m in range(6):
                relu_squared(0, 0, m, True)
                if m in (2, 5):
                    up_hi(1, m // 3, RAW_MLP + 32, 3 * (m // 3) + 3)

            def mlp_act(i, par, more):
                act.wait_ge(up_done, 6 * i + 7)
                for k in range(2):
                    down_hi(i, k, RAW_MLP + 32 * i + 48)
                for m in range(6):
                    relu_squared(i + 1, par, m)
                    if more and m in (2, 5):
                        up_hi(i + 2, m // 3, RAW_MLP + 32 * i + 64, 6 * i + 6 + m + 1)

            with act.Fori(0, (MLP_STEPS - 1) // 2) as j:
                for o in range(2):
                    mlp_act(2 * j + o, (o + 1) % 2, True)
            mlp_act(MLP_STEPS - 1, MLP_STEPS % 2, False)
            act.wait_ge(down_done, 2 * NT * MLP_STEPS)
            for k in range(2):
                down_hi(NFB - 1, k, RAW_MLP + 16 * 32)


        @block.vector
        def _(dve):
            d = Steps(dve, dve_step)

            def h2_of(dve, t):
                dve.wait_ge(x1_rs, t + 1)
                nc.vector.scalar_tensor_tensor(x_e[:, t % 2, :, :], mix[:, :, t * P:(t + 1) * P], x_rs[:, t:t + 1],
                                               ln2_b[:], ALU.mult, ALU.mult).then_inc(h2_ready, 1)

            nc.vector.memset(ah[:], 0.0).then_inc(mix_ready, 1)

            def x_mean_of(t):
                dve.wait_ge(x_squared, t + 1)
                nc.vector.tensor_scalar(x_ms[:, t:t + 1], x_ss[:, t:t + 1], 1.0 / D, EPS, ALU.mult, ALU.add).then_inc(x_mean, 1)

            def x_norm(t):
                dve.wait_ge(x_rstd, t + 1)
                nc.vector.scalar_tensor_tensor(x_in[:, t % 3, :], x_in[:, t % 3, :], x_rs[:, t:t + 1], ln1_b[:],
                                               ALU.mult, ALU.mult).then_inc(x_normed, 1)

            def turn_lo(t):
                for b in range(2):
                    dve.wait_ge(h_hi_ready, 2 * t + b + 1)
                    at = (slice(None), slice(4 * b, 4 * b + 4), slice(t * P, (t + 1) * P))
                    nc.vector.tensor_tensor(h_lo[at], psum[:, 2 * (t % 2) + b, :].rearrange("p (k n) -> p k n", k=4),
                                            h_hi[at].bitcast(F32), ALU.subtract).then_inc(h_lo_ready, 1)

            dve.wait_ge(small_in, 16 * SMALL)
            for t in range(NT):
                x_mean_of(t)
                if t == 2:
                    dve.wait_ge(rows_turned, 1)
                    nc.vector.tensor_copy(param[:, :, 0:ROWS], psum[:, 4, 0:LC * ROWS].rearrange(
                        "p (c r) -> p c r", c=LC)).then_inc(params_copied, 1)
                if t >= 1:
                    turn_lo(t - 1)
                x_norm(t)
            turn_lo(NT - 1)
            dve.wait_ge(wf_split, 1)
            nc.vector.tensor_tensor(wf_lo[:], wf_raw[:], wf_hi[:].bitcast(F32), ALU.subtract).then_inc(wf_ready, 1)

            def lru_lo(c, u):
                dve.wait_ge(w_hi, 2 * c + u + 1)
                nc.vector.tensor_tensor(wl_lo[:, u, :, :].rearrange("p k n -> p (k n)"), raw[:, u, :],
                                        wl_hi[:, u, :, :].rearrange("p k n -> p (k n)").bitcast(F32),
                                        ALU.subtract).then_inc(w_lo, 1)

            lru_lo(0, 0)
            lru_lo(0, 1)
            dve.wait_ge(f_turned, 1)
            d.did(nc.vector.tensor_tensor(l_in[:, 0:NT * H].rearrange("p (t h) -> p t h", h=H),
                                          psum[:, 4, 256:256 + NT * H].rearrange("p (t h) -> p t h", h=H),
                                          bf_b[:, None, :].to_broadcast([P, NT, H]), ALU.add))
            d.link(nc.vector.tensor_copy(l_in[:, NT * H:NL], param[:, :, R_LAM]))
            nc.vector.scalar_tensor_tensor(l_e[:], l_in[:], -1.0, l_in[:], ALU.mult, ALU.max).then_inc(l_abs, 1)
            dve.wait_ge(l_exp, 1)
            d.link(nc.vector.tensor_scalar(l_s[:], l_e[:], 2.0, None, ALU.add))
            d.link(nc.vector.reciprocal(l_q[:], l_s[:]))
            d.link(nc.vector.tensor_tensor(l_s[:], l_e[:], l_q[:], ALU.mult))
            d.link(nc.vector.tensor_tensor(l_q[:], l_s[:], l_s[:], ALU.mult))
            d.link(nc.vector.tensor_scalar(l_f[:], l_q[:], 1.0 / 15, None, ALU.mult))
            for odd in (13, 11, 9, 7, 5, 3):
                d.link(nc.vector.scalar_tensor_tensor(l_f[:], l_f[:], 1.0 / odd, l_q[:], ALU.add, ALU.mult))
            d.link(nc.vector.scalar_tensor_tensor(l_e[:], l_f[:], 1.0, l_s[:], ALU.add, ALU.mult))
            d.link(nc.vector.tensor_scalar(l_in[:], l_in[:], 0.0, None, ALU.min))
            nc.vector.scalar_tensor_tensor(l_f[:], l_e[:], -2.0, l_in[:], ALU.mult, ALU.add).then_inc(logf_ready, 1)
            dve.wait_ge(logf_ready, 1)
            nc.vector.tensor_scalar(param[:, :, R_SP4], l_f[:, NT * H:NL], -4.0, None, ALU.mult)
            nc.vector.tensor_scalar(param[:, :, R_NSP4], l_f[:, NT * H:NL], 4.0, None, ALU.mult)
            d.link(nc.vector.tensor_scalar(param[:, :, R_HBGA:R_HBGX + 1], param[:, :, R_BGA:R_BGX + 1], 0.5, None,
                                           ALU.mult))

            starts = slice(SEQ, T_ALL, DEC_T)

            def chunk(c, last):
                d.link(nc.vector.tensor_copy(pc[:], param[:, bass.ds(c, 1), :]))
                d.link(nc.vector.tensor_copy(spad[:, :, 0:3], pc[:, R_CONV:ROWS].rearrange("p (b j) -> p b j", b=DEC_B)))
                dve.wait_ge(xr_copied, 4 * c + 4)
                xcs = xc[:, SEQ:].rearrange("p (b t) -> p b t", b=DEC_B)
                d.did(nc.vector.tensor_scalar(xc[:, 0:SEQ], xpad[:, 3:], pc[:, 3:4], pc[:, R_CONVB:R_CONVB + 1],
                                              ALU.mult, ALU.add))
                d.link(nc.vector.tensor_scalar(xcs, spad[:, :, 3:], pc[:, 3:4], pc[:, R_CONVB:R_CONVB + 1],
                                               ALU.mult, ALU.add))
                for j in (2, 1, 0):
                    d.did(nc.vector.scalar_tensor_tensor(xc[:, 0:SEQ], xpad[:, j:j + SEQ], pc[:, j:j + 1], xc[:, 0:SEQ],
                                                         ALU.mult, ALU.add))
                    d.link(nc.vector.scalar_tensor_tensor(xcs, spad[:, :, j:j + DEC_T], pc[:, j:j + 1], xcs,
                                                          ALU.mult, ALU.add))
                nc.vector.tensor_copy(h_keep[:, bass.ds(c, 1), 9:12], xpad[:, None, SEQ:SEQ + 3])
                nc.vector.tensor_copy(h_keep[:, bass.ds(c, 1), 12:36].rearrange("p a (b j) -> p (a b) j", b=DEC_B),
                                      spad[:, :, DEC_T:]).then_inc(xc_ready, 1)
                if not last:
                    lru_lo(c + 1, 0)
                    lru_lo(c + 1, 1)
                dve.wait_ge(decays_ready, c + 1)
                nc.vector.scalar_tensor_tensor(a2[:], a2[:], 1.0, tl[:], ALU.add, ALU.mult).then_inc(one_minus_a2, 1)
                d.did(nc.vector.scalar_tensor_tensor(ti[:], ti[:], 1.0, xc[:], ALU.add, ALU.mult))
                d.link(nc.vector.tensor_tensor(ah[:], decay[:, starts], pc[:, R_H0:R_H0 + DEC_B], ALU.mult))
                dve.wait_ge(root_ready, c + 1)
                d.link(nc.vector.tensor_tensor(ti[:], ti[:], tr[:], ALU.mult))
                d.did(nc.vector.tensor_tensor(ti[:, starts], ti[:, starts], ah[:], ALU.add))
                d.link(nc.vector.memset(decay[:, starts], 0.0))
                d.link(nc.vector.tensor_tensor_scan(tl[:], decay[:], ti[:], 0.0, ALU.mult, ALU.add))
                nc.vector.tensor_copy(h_keep[:, bass.ds(c, 1), 0:1], tl[:, None, SEQ - 1:SEQ])
                nc.vector.tensor_copy(h_keep[:, bass.ds(c, 1), 1:9], tl[:, None, SEQ + DEC_T - 1:T_ALL:DEC_T])
                nc.vector.tensor_tensor(mix[:, bass.ds(c + LC, 1), :].rearrange("p a n -> p (a n)"), gy[:], tl[:],
                                        ALU.mult).then_inc(mix_ready, 1)

            dve.wait_ge(consts_ready, 2)
            before = d.n
            with dve.Fori(0, LC - 1) as c:
                d.enter(c, DVE_LRU, before)
                chunk(c, False)
                d.leave(DVE_LRU, before, LC - 1)
            nc.vector.tensor_tensor(lf_own[:], l_f[:, None, (NT - 1) * H:NT * H].to_broadcast([P, DEC_B, H]),
                                    block_of[:, :, None].to_broadcast([P, DEC_B, H]), ALU.mult).then_inc(c_own_ready, 1)
            dve.wait_ge(c_turned, 1)
            d.link(nc.vector.tensor_tensor_scan(cp[:, 0:512], ones_w[0:H, :], psum[0:H, 3, :], 0.0, ALU.mult, ALU.add))
            d.did(nc.vector.tensor_tensor_scan(cp[:, 512:], ones_w[0:H, :], psum[0:H, 4, :], cp[:, 511:512],
                                               ALU.mult, ALU.add))
            d.did(nc.vector.tensor_tensor_scan(cc[:, 0:PAST], ones_w[:], psum[0:64, 5, :], 0.0, ALU.mult, ALU.add))
            dve.wait_ge(c_turned, 2)
            d.link(nc.vector.reduce_sum(c_new[:], psum[0:64, 6, 0:P].rearrange("p (b t) -> p t b", b=DEC_B), AX_X))
            d.link(nc.vector.tensor_tensor_scan(cc_new[:], ones_w[:, 0:DEC_T], c_new[:], cc[:, PAST - 1:PAST],
                                                ALU.mult, ALU.add))
            nc.vector.tensor_copy(cc[:, PAST:].rearrange("p (b t) -> p b t", b=DEC_B),
                                  cc_new[:, None, :].to_broadcast([64, DEC_B, DEC_T])).then_inc(c_read, 1)
            dve.wait_ge(c_read, 1)
            for c_all, mid, hi_at, mid_at, lo_at in (
                    (cc, c_mid, c_past[0:64, 0, :], c_past[64:P, 0, :], c_past[0:64, 1, :]),
                    (cp, cp_mid, c_prompt[0:H, :], c_prompt[32:32 + H, :], c_prompt[64:64 + H, :])):
                d.link(nc.vector.tensor_scalar(hi_at, c_all[:], -1.0, None, ALU.mult))
                d.link(nc.vector.scalar_tensor_tensor(c_all[:], c_all[:], -1.0, hi_at, ALU.mult, ALU.subtract))
                d.link(nc.vector.tensor_copy(mid[:], c_all[:]))
                d.did(nc.vector.tensor_copy(mid_at, mid[:]))
                d.link(nc.vector.tensor_tensor(c_all[:], c_all[:], mid[:], ALU.subtract))
                d.link(nc.vector.tensor_copy(lo_at, c_all[:]))
            nc.vector.memset(c_new[:, 0:1], 0.0).then_inc(c_ready, 1)
            extra = d.n - before - DVE_LRU * (LC - 1)
            d.enter(LC - 1, DVE_LRU, before + extra)
            chunk(LC - 1, True)
            d.leave(DVE_LRU, before + extra, LC)
            nc.vector.tensor_scalar(qgain[:], qgain[:], DH ** -0.5, None, ALU.mult)
            d.link(nc.vector.memset(q_blocks[:], 0.0))

            def pair_lo(p, j):
                dve.wait_ge(w_hi, 2 * LC + 4 * p + j + 1)
                nc.vector.tensor_tensor(wp_lo[:, 2 * j:2 * j + 2, :].rearrange("p k n -> p (k n)"), raw[:, j % 2, 0:2 * PW3],
                                        wp_hi[:, 2 * j:2 * j + 2, :].rearrange("p k n -> p (k n)").bitcast(F32),
                                        ALU.subtract).then_inc(w_lo, 1)

            for j in range(4):
                pair_lo(0, j)

            def pair_dve(p, last):
                def mean(t):
                    dve.wait_ge(pair_sq, NT * p + t + 1)
                    d.link(nc.vector.reduce_sum(s4[:, t % 2, :], sqj[:].rearrange("p (a d) -> p a d", d=DH), AX_X))
                    nc.vector.tensor_scalar(m4[:, t % 2, :], s4[:, t % 2, :], 1.0 / DH, EPS, ALU.mult,
                                            ALU.add).then_inc(s4_ready, 1)

                def norm(t):
                    dve.wait_ge(rs4_ready, NT * p + t + 1)
                    if t >= 3:
                        dve.wait_ge(qk_turned, NT * p + t - 2)
                        dve.wait_ge(k_out[t % 3], 48 * p + 16 * (t // 3))
                    v = qk[:, t % 3, :].rearrange("p (a d) -> p a d", d=DH)
                    d.link(nc.vector.tensor_tensor(v, psum[:, PB[t % 3], 0:2 * P].rearrange("p (a d) -> p a d", d=DH),
                                                   rs4[:, t % 2, :, None].to_broadcast([P, 4, DH]), ALU.mult))
                    nc.vector.tensor_tensor(v[:, 2:4, :], v[:, 2:4, :], kgain[:, None, :].to_broadcast([P, 2, DH]),
                                            ALU.mult).then_inc(qk_ready, 1)

                def k_turn_out(g):
                    n = SPAN if g < 2 else P
                    dve.wait_ge(qk_turned, NT * p + min(4 * g + 4, NT))
                    nc.vector.tensor_copy(kt_all[:, g * SPAN:g * SPAN + n], psum[:, KB[g], 0:n]).then_inc(k_done, 1)

                mean(0)
                for t in range(NT):
                    if t < NT - 1:
                        mean(t + 1)
                    norm(t)
                    if t == 6:
                        k_turn_out(0)
                k_turn_out(1)
                k_turn_out(2)
                for hp in range(2):
                    r = slice(hp * DH, (hp + 1) * DH)
                    dve.wait_ge(q_done, 3 * p + 3)
                    nc.vector.tensor_copy(q_blocks[r, :, hp, :], qt[r, SEQ:].rearrange("p (b q) -> p b q", b=DEC_B)
                                          ).then_inc(q_blocks_ready, 1)

                def top_of(s):
                    nk = 4 * step_of(s)[1] + step_of(s)[2] + 1
                    dve.wait_ge(scores, 16 * p + s + 1)
                    d.link(nc.vector.reduce_max(top[:, s % 2:s % 2 + 1], two_banks(SB[s % 2])[:, 0:nk * P], AX_X))
                    nc.vector.tensor_scalar(neg_top[:, s % 2:s % 2 + 1], top[:, s % 2:s % 2 + 1], -1.0, None,
                                            ALU.mult).then_inc(top_ready, 1)

                def turned_b(s):
                    hp, g, j = step_of(s)
                    if g == 1:
                        dve.wait_ge(p_turned, 16 * p + s + 1)
                        nc.vector.tensor_copy(pts[:, 4:4 + j + 1, j * P:(j + 1) * P],
                                              psum[:, 3, 0:(j + 1) * P].rearrange("p (k n) -> p k n", n=P)).then_inc(pt_b, 1)

                def share(s, n, done, count):
                    dve.wait_ge(done, count)
                    d.link(nc.vector.reciprocal(rden[:, s % 2:s % 2 + 1], den[:, s % 2:s % 2 + 1]))
                    return nc.vector.tensor_scalar(probs[:, s % 2, 0:n], probs[:, s % 2, 0:n], rden[:, s % 2:s % 2 + 1],
                                                   None, ALU.mult)

                top_of(0)
                for s in range(16):
                    if s >= 1:
                        turned_b(s - 1)
                    if s < 15:
                        top_of(s + 1)
                    share(s, (4 * step_of(s)[1] + step_of(s)[2] + 1) * P, exp_done, 16 * p + s + 1).then_inc(probs_ready, 1)
                    if not last and s in (4, 6, 8, 10):
                        pair_lo(p + 1, (s - 4) // 2)
                turned_b(15)
                for b in range(1, DEC_B, 2):
                    dve.wait_ge(kc_turned, DEC_B * p + b + 1)
                    nc.vector.tensor_copy(pts[:, 3, :], psum[:, 3, :]).then_inc(kts_b, 1)
                for g in range(2):
                    dve.wait_ge(s_scores, 2 * p + g + 1)
                    d.link(nc.vector.reduce_max(top[:, g:g + 1], two_banks(SB[g])[:, 0:KEYS], AX_X))
                    nc.vector.tensor_scalar(neg_top[:, g:g + 1], top[:, g:g + 1], -1.0, None, ALU.mult).then_inc(s_top, 1)
                for g in range(2):
                    share(g, KEYS, s_exp, 2 * p + g + 1).then_inc(s_probs, 1)
                for g in range(2):
                    dve.wait_ge(s_turned, 2 * p + g + 1)
                    nc.vector.tensor_copy(pts[:, 1, 0:P], psum[:, 3, 0:P]).then_inc(s_ptb, 1)

            before = d.n
            with dve.Fori(0, PAIRS - 1) as p:
                d.enter(p, DVE_PAIR, before)
                pair_dve(p, False)
                d.leave(DVE_PAIR, before, PAIRS - 1)
            d.enter(PAIRS - 1, DVE_PAIR, before)
            pair_dve(PAIRS - 1, True)
            d.leave(DVE_PAIR, before, PAIRS)
            def tile(t):
                return slice(t * P, (t + 1) * P)

            def mix_sums_of(t):
                dve.wait_ge(mix_sq, t + 1)
                nc.vector.reduce_sum(ssq[:], sq[:].rearrange("p (a k) n -> p a n k", a=2), AX_X).then_inc(mix_ssq, 1)
                dve.wait_ge(mix_sums, t + 1)
                nc.vector.tensor_scalar(ms2[:, t % 2, :], psum[:, 6, 0:2], 1.0 / LW, EPS, ALU.mult, ALU.add).then_inc(mix_ms, 1)

            def mix_lo_of(t):
                dve.wait_ge(mix_hi, t + 1)
                nc.vector.tensor_tensor(h_lo[:, :, tile(t)], mix[:, :, tile(t)], h_hi[:, :, tile(t)].bitcast(F32),
                                        ALU.subtract).then_inc(mix_lo, 1)

            for j in range(KC):
                r = R_GAO if j < LC else R_GLO
                dve.wait_ge(w_hi, V_OUT + j + 1)
                nc.vector.scalar_tensor_tensor(wo_lo[:, j, :], raw[:, j % 2, :], param[:, j % LC, r:r + 1],
                                               wo_hi[:, j, :].bitcast(F32), ALU.mult, ALU.subtract).then_inc(w_lo, 1)
                if j == 1:
                    mix_sums_of(0)
                    mix_lo_of(0)
            dve.wait_ge(ln2_in, 16)
            for t in range(NT):
                if t < NT - 1:
                    mix_sums_of(t + 1)
                    mix_lo_of(t + 1)
                else:
                    for c in range(2):
                        dve.wait_ge(w_hi, V_MLP + c + 1)
                        nc.vector.tensor_tensor(wu_lo[:, c, :, :].rearrange("p k n -> p (k n)"), raw[:, c, :],
                                                wu_hi[:, c, :, :].rearrange("p k n -> p (k n)").bitcast(F32),
                                                ALU.subtract).then_inc(w_lo, 1)
                dve.wait_ge(xe_in[t % 2], 16 * (t // 2) + 16)
                dve.wait_ge(mix_rs, t + 1)
                for half in range(2):
                    dve.wait_ge(out_done, 2 * t + half + 1)
                    at = mix[:, 4 * half:4 * half + 4, tile(t)]
                    if half == 0:
                        dve.wait_ge(mix_lo, t + 1)
                    d.link(nc.vector.scalar_tensor_tensor(
                        at, psum[:, 2 * half, :].rearrange("p (k n) -> p k n", n=P), rs2[:, t % 2, 0:1],
                        x_e[:, t % 2, 4 * half:4 * half + 4, :], ALU.mult, ALU.add))
                    last = nc.vector.scalar_tensor_tensor(
                        at, psum[:, 2 * half + 1, :].rearrange("p (k n) -> p k n", n=P), rs2[:, t % 2, 1:2], at,
                        ALU.mult, ALU.add)
                    if half == 0:
                        d.link(last)
                last.then_inc(x1_ready, 1)
                dve.wait_ge(x1_sq, t + 1)
                nc.vector.tensor_scalar(x_ms[:, t:t + 1], x_ss[:, t:t + 1], 1.0 / D, EPS, ALU.mult, ALU.add).then_inc(x1_ms, 1)
                for u in ([t - 1] if t else []) + ([t] if t == NT - 1 else []):
                    if u == t:
                        h2_of(dve, t)
                    for b in range(2):
                        dve.wait_ge(h2_hi, 2 * u + b + 1)
                        at = (slice(None), slice(4 * b, 4 * b + 4), tile(u))
                        nc.vector.tensor_tensor(h_lo[at], psum[:, 4 + b, :].rearrange("p (k n) -> p k n", k=4),
                                                h_hi[at].bitcast(F32), ALU.subtract).then_inc(h2_lo, 1)
                if t < NT - 1:
                    h2_of(dve, t)

            for bank in range(4):
                nc.vector.tensor_copy(x_ms[:, 0:1], x_ms[:, 1:2]).then_inc(y_added, 1)
                dve.wait_ge(y_added, bank + 1)

            def up_lo(c, unit):
                dve.wait_ge(w_hi, unit + 1)
                nc.vector.tensor_tensor(wu_lo[:, c, :, :].rearrange("p k n -> p (k n)"), raw[:, c, :],
                                        wu_hi[:, c, :, :].rearrange("p k n -> p (k n)").bitcast(F32),
                                        ALU.subtract).then_inc(w_lo, 1)

            def down_lo(k, unit):
                dve.wait_ge(w_hi, unit + 1)
                nc.vector.tensor_tensor(wd_lo[:, k, :], raw[:, k, :], wd_hi[:, k, :].bitcast(F32),
                                        ALU.subtract).then_inc(w_lo, 1)

            def split_u(b, par, m):
                dve.wait_ge(up_squared, 6 * b + m + 1)
                at = (slice(None), par, m // 3, slice((m % 3) * GN, (m % 3 + 1) * GN))
                d.link(nc.vector.tensor_copy(u_hi[at], up[:, m % 3, :]))
                nc.vector.tensor_tensor(u_lo[at], up[:, m % 3, :], u_hi[at].bitcast(F32), ALU.subtract).then_inc(u_ready, 1)

            def add_y(i):
                for t in range(NT):
                    for half in range(2):
                        dve.wait_ge(down_done, 2 * NT * i + 2 * t + half + 1)
                        at = mix[:, 4 * half:4 * half + 4, tile(t)]
                        nc.vector.tensor_tensor(at, psum[:, 4 + 2 * (t % 2) + half, :].rearrange("p (k n) -> p k n", n=P), at,
                                                ALU.add).then_inc(y_added, 1)

            for m in range(6):
                split_u(0, 0, m)
                if m in (2, 5):
                    up_lo(m // 3, V_MLP + 2 + m // 3)

            def mlp_dve(i, par, more):
                for k in range(2):
                    down_lo(k, V_MLP + 4 * i + 4 + k)
                for m in range(6):
                    split_u(i + 1, par, m)
                    if more and m in (2, 5):
                        up_lo(m // 3, V_MLP + 4 * i + 6 + m // 3)
                add_y(i)

            before = d.n
            with dve.Fori(0, (MLP_STEPS - 1) // 2) as j:
                d.enter(j, 12, before)
                for o in range(2):
                    mlp_dve(2 * j + o, (o + 1) % 2, True)
                d.leave(12, before, (MLP_STEPS - 1) // 2)
            mlp_dve(MLP_STEPS - 1, MLP_STEPS % 2, False)
            for k in range(2):
                down_lo(k, V_MLP + 4 * MLP_STEPS + 2 + k)
            add_y(NFB - 1)

        @block.tensor
        def _(pe):
            def split_product(out, hi, lo, r_hi, r_lo, n, first=True, end=True):
                for k in range(n):
                    nc.tensor.matmul(out, hi(k), r_hi(k), start=first and k == 0, stop=False)
                    nc.tensor.matmul(out, hi(k), r_lo(k), start=False, stop=False)
                    last = nc.tensor.matmul(out, lo(k), r_hi(k), start=False, stop=end and k == n - 1)
                return last

            pe.wait_ge(consts_ready, 1)

            def turn(t):
                pe.wait_ge(x_normed, t + 1)
                if t >= 2:
                    pe.wait_ge(h_lo_ready, 2 * (t - 2) + 2)
                for b in range(2):
                    for k in range(4):
                        last = nc.tensor.transpose(psum[:, 2 * (t % 2) + b, k * P:(k + 1) * P],
                                                   x_in[:, t % 3, (4 * b + k) * P:(4 * b + k + 1) * P], ident[:])
                    last.then_inc(x_turned, 1)

            pe.wait_ge(small_in, 16 * SMALL)
            for c in range(LC):
                last = nc.tensor.transpose(psum[:, 4, c * ROWS:(c + 1) * ROWS], rows[:, c * P:(c + 1) * P],
                                           ident[0:ROWS, 0:ROWS])
            last.then_inc(rows_turned, 1)
            for t in range(NT):
                turn(t)
            pe.wait_ge(wf_ready, 1)
            pe.wait_ge(h_lo_ready, 2 * NT)
            for g in range(G):
                n = slice(g * GN, (g + 1) * GN)
                split_product(psum[0:H, 5 + g, 0:GN], lambda k: wf_hi[:, k, :], lambda k: wf_lo[:, k, :],
                              lambda k: h_hi[:, k, n], lambda k: h_lo[:, k, n], KC).then_inc(f_done, 1)
            pe.wait_ge(f_copied, G)
            pe.wait_ge(params_copied, 1)
            for t in range(NT):
                last = nc.tensor.transpose(psum[:, 4, 256 + t * H:256 + (t + 1) * H], f_rows[:, t * P:(t + 1) * P],
                                           ident[0:H, 0:H])
            last.then_inc(f_turned, 1)

            def chunk(c, last_chunk):
                for u in range(2):
                    pe.wait_ge(w_lo, 2 * c + u + 1)
                    if u == 1 and last_chunk:
                        pe.wait_ge(c_read, 1)
                    for g in range(G):
                        n = slice(g * GN, (g + 1) * GN)
                        split_product(psum[:, 3 * u + g, 0:GN], lambda k: wl_hi[:, u, k, :], lambda k: wl_lo[:, u, k, :],
                                      lambda k: h_hi[:, k, n], lambda k: h_lo[:, k, n], KC).then_inc(proj_done, 1)
                pe.wait_ge(xc_ready, c + 1)
                pe.wait_ge(gw_in, 64 * c + 64)
                for m in range(6):
                    g = m % 3
                    if m >= 2:
                        pe.wait_ge(gate_read, 6 * c + m - 1)
                    nc.tensor.matmul(psum[:, 6 + m % 2, 0:GN], gate_w[:, m // 3, :], xc[:, g * GN:(g + 1) * GN],
                                     start=True, stop=True).then_inc(gate_done, 1)

            pe.wait_ge(l_abs, 1)
            with pe.Fori(0, LC - 1) as c:
                chunk(c, False)
            pe.wait_ge(gate_read, 6 * (LC - 1))
            pe.wait_ge(logf_ready, 1)
            for t in range(SEQ // P):
                nc.tensor.transpose(psum[0:H, 3 + t // 4, (t % 4) * P:(t % 4 + 1) * P], l_f[:, t * H:(t + 1) * H], ident[:])
            for kt in range(KP):
                last = nc.tensor.transpose(psum[0:64, 5, kt * P:(kt + 1) * P], cl[:, kt, :], ident[:])
            last.then_inc(c_turned, 1)
            pe.wait_ge(c_own_ready, 1)
            nc.tensor.matmul(psum[0:64, 6, 0:P], lf_own[:].rearrange("p b h -> p (b h)"), ident[:],
                             start=True, stop=True).then_inc(c_turned, 1)
            chunk(LC - 1, True)
            pe.wait_ge(gate_read, 6 * LC)

            def pair_pe(p):
                pe.wait_ge(w_lo, 2 * LC + 4 * p + 4)
                pe.wait_ge(s_out, p + 1)

                def turn_qk(t):
                    pe.wait_ge(qk_ready, NT * p + t + 1)
                    if t == NT - 1:
                        pe.wait_ge(q_done, 3 * p + 1)
                        pe.wait_ge(k_done, 3 * p + 1)
                    at = slice((t % 4) * P, (t % 4 + 1) * P)
                    nc.tensor.transpose(psum[:, QB[t // 4], at], qk[:, t % 3, 0:P], ident[:])
                    nc.tensor.transpose(psum[:, KB[t // 4], at], qk[:, t % 3, P:2 * P], ident[:]).then_inc(qk_turned, 1)

                for t in range(NT):
                    if t >= 3:
                        pe.wait_ge(qk_ready, NT * p + t - 2)
                        pe.wait_ge(v_done, NT * p + t - 2)
                    n = slice(t * P, (t + 1) * P)
                    split_product(psum[:, PB[t % 3], 0:PW3], lambda k: h_hi[:, k, n], lambda k: h_lo[:, k, n],
                                  lambda k: wp_hi[:, k, :], lambda k: wp_lo[:, k, :], KC).then_inc(pair_proj, 1)
                    if t >= 2:
                        turn_qk(t - 2)
                turn_qk(NT - 2)
                turn_qk(NT - 1)
                pe.wait_ge(q_done, 3 * p + 3)
                pe.wait_ge(k_done, 3 * p + 3)
                pe.wait_ge(v_done, NT * p + NT)

                def score(s):
                    hp, g, j = step_of(s)
                    nk = 4 * g + j + 1
                    if s >= 2:
                        pe.wait_ge(exp_done, 16 * p + s - 1)
                    r = slice(hp * DH, (hp + 1) * DH)
                    for part in range((nk + 3) // 4):
                        n = min(nk - 4 * part, 4) * P
                        out = psum[:, SB[s % 2] + part, 0:n]
                        keys = slice(part * SPAN, part * SPAN + n)
                        nc.tensor.matmul(out, e_head[:, bass.ds(2 * p + hp, 1), :].rearrange("p a m -> p (a m)"),
                                         c_prompt[:, keys], start=True, stop=False)
                        if part == g:
                            nc.tensor.matmul(psum[:, SB[s % 2] + part, j * P:(j + 1) * P], ident_b[:], cmask[:],
                                             start=False, stop=False)
                        last = nc.tensor.matmul(out, qt[r, (4 * g + j) * P:(4 * g + j + 1) * P], kt_all[r, keys],
                                                start=False, stop=True)
                    last.then_inc(scores, 1)

                def turn_probs(s):
                    hp, g, j = step_of(s)
                    pe.wait_ge(probs_ready, 16 * p + s + 1)
                    if s >= 1:
                        pe.wait_ge(pt_a, 16 * p + s)
                    if g == 1 and (s // 8, j) != (0, 0):
                        pe.wait_ge(pt_b, 8 * p + 4 * hp + j)
                    for kt in range(4 * g + j + 1):
                        last = nc.tensor.transpose(psum[:, 2 + kt // 4, (kt % 4) * P:(kt % 4 + 1) * P],
                                                   probs[:, s % 2, kt * P:(kt + 1) * P], ident[:])
                    last.then_inc(p_turned, 1)

                def values(gi):
                    hp, g = gi // 2, gi % 2
                    r = slice(hp * DH, (hp + 1) * DH)
                    pe.wait_ge(pt_a, 16 * p + 4 * gi + 4)
                    if g == 1:
                        pe.wait_ge(pt_b, 8 * p + 4 * hp + 4)
                    if gi >= 2:
                        pe.wait_ge(o_done, 4 * p + gi - 1)
                    for kt in range(4 * g + 4):
                        n = slice(max(kt - 4 * g, 0) * P, SPAN)
                        last = nc.tensor.matmul(psum[r, gi % 2, n], vt[:, kt, r], pts[:, kt, n],
                                                start=kt == 0, stop=kt == 4 * g + 3)
                    last.then_inc(pv_done, 1)

                score(0)
                for s in range(16):
                    if s < 15:
                        score(s + 1)
                    turn_probs(s)
                    if s % 4 == 3:
                        values(s // 4)

                pe.wait_ge(q_blocks_ready, 2 * p + 2)
                pe.wait_ge(pt_a, 16 * p + 16)
                pe.wait_ge(pt_b, 8 * p + 8)
                pe.wait_ge(exp_done, 16 * p + 16)

                def turn_past(b):
                    pe.wait_ge(kc_in[b % 2], 64 * p + 16 * (b // 2) + 16)
                    if b >= 2:
                        pe.wait_ge((kts_a, kts_b)[b % 2], 4 * p + b // 2)
                    for kt in range(KP):
                        last = nc.tensor.transpose(psum[:, 2 + b % 2, kt * P:(kt + 1) * P], k_c[:, b % 2, kt, :], ident[:])
                    last.then_inc(kc_turned, 1)

                def score_stream(b):
                    g, r = b // 4, slice((b % 4) * 32, (b % 4 + 1) * 32)
                    past, new = psum[:, SB[g], 0:PAST], psum[:, SB[g] + 1, 0:P]
                    if b % 4 == 0:
                        rows_of = e_row[:, bass.ds(2 * p + g, 1), :].rearrange("p a m -> p (a m)")
                        nc.tensor.matmul(past, rows_of, c_past[:, 0, 0:PAST], start=True, stop=False)
                        nc.tensor.matmul(past, rows_of, c_past[:, 1, 0:PAST], start=False, stop=False)
                        nc.tensor.matmul(new, rows_of, c_past[:, 0, PAST:], start=True, stop=False)
                        nc.tensor.matmul(new, rows_of, c_past[:, 1, PAST:], start=False, stop=False)
                        nc.tensor.matmul(new, ident_b[:], smask[:, g, :], start=False, stop=False)
                    pe.wait_ge((kts_a, kts_b)[b % 2], 4 * p + b // 2 + 1)
                    q = q_blocks[:, b, :, :].rearrange("p h q -> p (h q)")
                    nc.tensor.matmul(psum[r, SB[g], 0:PAST], q, pts[:, 2 + b % 2, :], start=False, stop=True)
                    last = nc.tensor.matmul(psum[r, SB[g] + 1, 0:P], q, kt_all[:, SEQ:], start=False, stop=True)
                    if b % 4 == 3:
                        last.then_inc(s_scores, 1)

                turn_past(0)
                for b in range(DEC_B):
                    if b < DEC_B - 1:
                        turn_past(b + 1)
                    score_stream(b)
                pe.wait_ge(o_done, 4 * p + 4)
                for g in range(2):
                    pe.wait_ge(s_probs, 2 * p + g + 1)
                    if g == 1:
                        pe.wait_ge(s_pta, 2 * p + 1)
                        pe.wait_ge(s_ptb, 2 * p + 1)
                    for kt in range(KP):
                        nc.tensor.transpose(psum[:, 2, kt * P:(kt + 1) * P], probs[:, g, kt * P:(kt + 1) * P], ident[:])
                    nc.tensor.transpose(psum[:, 3, 0:P], probs[:, g, PAST:KEYS], ident[:]).then_inc(s_turned, 1)
                    pe.wait_ge(s_ptb, 2 * p + g + 1)
                    pe.wait_ge(s_pta, 2 * p + g + 1)
                    nc.tensor.matmul(psum[:, g, 0:P], vt[:, NT - 1, :], pts[:, 1, 0:P], start=True, stop=False)
                    for b in range(4):
                        pe.wait_ge(vc_in[b], 32 * p + 16 * g + 16)
                        for kt in range(KP):
                            last = nc.tensor.matmul(psum[:, g, b * 32:(b + 1) * 32], v_c[:, b, kt, :],
                                                    pts[:, 0, kt * P + b * 32:kt * P + (b + 1) * 32],
                                                    start=False, stop=b == 3 and kt == KP - 1)
                    last.then_inc(s_pv, 1)

            with pe.Fori(0, PAIRS) as p:
                pair_pe(p)
            def tile(t):
                return slice(t * P, (t + 1) * P)

            def sums(t):
                pe.wait_ge(mix_ssq, t + 1)
                if t >= 1:
                    pe.wait_ge(mix_ms, t)
                for a in range(2):
                    last = nc.tensor.matmul(psum[:, 6, a:a + 1], ssq[:, a, :], ones_col[:], start=True, stop=True)
                last.then_inc(mix_sums, 1)

            def turn_h2(t):
                pe.wait_ge(h2_ready, t + 1)
                if t >= 1:
                    pe.wait_ge(h2_lo, 2 * t)
                for b in range(2):
                    for k in range(4):
                        last = nc.tensor.transpose(psum[:, 4 + b, k * P:(k + 1) * P], x_e[:, t % 2, 4 * b + k, :], ident[:])
                    last.then_inc(h2_turned, 1)

            pe.wait_ge(s_out, PAIRS + 1)
            for c in range(LC):
                last = nc.tensor.transpose(psum[0:36, 7, c * P:(c + 1) * P], h_keep[:, c, :], ident[:])
            last.then_inc(kept_turned, 1)
            sums(0)
            for t in range(NT):
                if t < NT - 1:
                    sums(t + 1)
                pe.wait_ge(mix_lo, t + 1)
                if t >= 1:
                    pe.wait_ge(x1_ready, t)
                for half in range(2):
                    for part in range(2):
                        if t == 0 and half == 0:
                            pe.wait_ge(w_lo, V_OUT + 4 * part + 4)
                        n = slice(half * SPAN, (half + 1) * SPAN)
                        last = split_product(psum[:, 2 * half + part, :],
                                             lambda k: h_hi[:, 4 * part + k, tile(t)], lambda k: h_lo[:, 4 * part + k, tile(t)],
                                             lambda k: wo_hi[:, 4 * part + k, n], lambda k: wo_lo[:, 4 * part + k, n], 4)
                    last.then_inc(out_done, 1)
                if t >= 1:
                    turn_h2(t - 1)
            turn_h2(NT - 1)

            def mlp_up(b, par, lo_ready, first=False):
                for c in range(2):
                    pe.wait_ge(w_lo, lo_ready + c)
                    for g in range(G):
                        m = 3 * c + g
                        if not (first and m < 4):
                            pe.wait_ge(up_read, 6 * b + m - 3)
                        n = slice(g * GN, (g + 1) * GN)
                        split_product(psum[:, up_bank(par, m), 0:GN], lambda k: wu_hi[:, c, k, :], lambda k: wu_lo[:, c, k, :],
                                      lambda k: h_hi[:, k, n], lambda k: h_lo[:, k, n], KC).then_inc(up_done, 1)

            def mlp_down(i, par, lo_ready):
                pe.wait_ge(u_ready, 6 * i + 6)
                pe.wait_ge(w_lo, lo_ready)
                for t in range(NT):
                    for half in range(2):
                        pe.wait_ge(y_added, 2 * NT * i + 2 * t + half + 1)
                        n = slice(half * SPAN, (half + 1) * SPAN)
                        split_product(psum[:, 4 + 2 * (t % 2) + half, :],
                                      lambda k: u_hi[:, par, k, tile(t)], lambda k: u_lo[:, par, k, tile(t)],
                                      lambda k: wd_hi[:, k, n], lambda k: wd_lo[:, k, n], 2).then_inc(down_done, 1)

            pe.wait_ge(h2_lo, 2 * NT)
            pe.wait_ge(kept_copied, 1)
            mlp_up(0, 0, V_MLP + 1, True)
            with pe.Fori(0, (MLP_STEPS - 1) // 2) as j:
                for o in range(2):
                    i = 2 * j + o
                    mlp_up(i + 1, (o + 1) % 2, V_MLP + 4 * i + 3)
                    mlp_down(i, o, V_MLP + 4 * i + 6)
            mlp_up(NFB - 1, (NFB - 1) % 2, V_MLP + 4 * (NFB - 2) + 3)
            mlp_down(NFB - 2, (NFB - 2) % 2, V_MLP + 4 * (NFB - 2) + 6)
            mlp_down(NFB - 1, (NFB - 1) % 2, V_MLP + 4 * (NFB - 1) + 4)
    ctx.close()


_INS = ["x_prompt", "x_sample", "cache_k", "cache_v", "cache_logf", "state_h", "state_conv", "ln1", "w_in", "b_f",
        "q_gain", "k_gain", "conv_w", "conv_b", "w_gate_a", "b_gate_a", "w_gate_x", "b_gate_x", "lru_lambda",
        "g_attn_out", "g_lru_out", "w_out", "ln2", "w_up", "w_down"]
_OUTS = [(1, SEQ, D), (DEC_B, DEC_T, D), (1, 1, SEQ, H, DH), (1, 1, SEQ, H, DH), (1, 1, SEQ, H), (1, 1, LW),
         (1, 1, CW - 1, LW), (1, DEC_B, DEC_T, H, DH), (1, DEC_B, DEC_T, H, DH), (1, DEC_B, DEC_T, H),
         (1, DEC_B, LW), (1, DEC_B, CW - 1, LW)]


def kernel(**inputs):
    from concourse import bacc
    from concourse.bass_utils import run_bass_kernel_spmd

    arrays = {f"in_{name}_dram": np.ascontiguousarray(np.asarray(inputs[name])) for name in _INS}
    nc = bacc.Bacc("TRN2", target_bir_lowering=False, num_devices=1)
    ins = [nc.dram_tensor(f"in_{name}_dram", list(arrays[f"in_{name}_dram"].shape), F32, kind="ExternalInput")
           for name in _INS]
    outs = [nc.dram_tensor(f"out_{i}_dram", list(shape), F32, kind="ExternalOutput") for i, shape in enumerate(_OUTS)]
    streaming_step(nc, *[t.ap() for t in ins], *[t.ap() for t in outs])
    nc.compile()
    results = run_bass_kernel_spmd(nc, [arrays], core_ids=[0]).results[0]
    return tuple(np.asarray(results[f"out_{i}_dram"]) for i in range(len(_OUTS)))
```

```python
from contextlib import ExitStack

import numpy as np

import concourse.bass as bass
from concourse import mybir

F32 = mybir.dt.float32
F32R = mybir.dt.float32r
BF16 = mybir.dt.bfloat16
ALU = mybir.AluOpType
ACT = mybir.ActivationFunctionType
AX_X = mybir.AxisListType.X

P = 128
D = 1024
SEQ = 1024
DEC_B = 8
DEC_T = 16
PAST = 512
H = 8
DH = 64
AW = H * DH
LW = D - AW
FF = 4 * D
CW = 4
EPS = 1e-6
T_ALL = SEQ + DEC_B * DEC_T
NT = T_ALL // P
KC = D // P
G = 3
GN = T_ALL // G
LC = LW // P
PAIRS = H // 2
MASKED = -(2.0 ** 100)
F_COL = 3 * AW
XR_COL = F_COL + H
YG_COL = XR_COL + LW
ROWS = 42
R_CONVW, R_CONVB, R_BGA, R_BGX, R_LAM, R_GAO, R_GLO, R_H0, R_CONV = 0, 4, 5, 6, 7, 8, 9, 10, 18
R_SP4, R_NSP4, R_HBGA, R_HBGX = 42, 43, 44, 45
PW = 46
KP = PAST // P
KEYS = PAST + P
FB = 256
NFB = FF // FB


def streaming_step(nc, x_prompt, x_sample, cache_k, cache_v, cache_logf, state_h, state_conv, ln1, w_in, b_f,
                   q_gain, k_gain, conv_w, conv_b, w_gate_a, b_gate_a, w_gate_x, b_gate_x, lru_lambda,
                   g_attn_out, g_lru_out, w_out, ln2, w_up, w_down,
                   y_prompt, y_sample, k_prompt, v_prompt, logf_prompt, h_prompt, conv_prompt,
                   k_sample, v_sample, logf_sample, h_sample, conv_sample):
    ctx = ExitStack()

    def sem(name):
        return ctx.enter_context(nc.semaphore(name))

    def sb(scope, name, shape, dt=F32):
        return scope.enter_context(nc.sbuf_tensor(name, shape, dt))

    h_hi = sb(ctx, "h_hi", [P, KC, T_ALL], F32R)
    h_lo = sb(ctx, "h_lo", [P, KC, T_ALL], F32R)
    mix = sb(ctx, "mix", [P, KC, T_ALL])
    ident = sb(ctx, "ident", [P, P])
    ones_col = sb(ctx, "ones_col", [P, 1])
    neg_half = sb(ctx, "neg_half", [P, 4])
    param = sb(ctx, "param", [P, LC, PW])
    x_ss = sb(ctx, "x_ss", [P, NT])
    x_ms = sb(ctx, "x_ms", [P, NT])
    x_rs = sb(ctx, "x_rs", [P, NT])

    h_keep = sb(ctx, "h_keep", [P, LC, 36])
    raw = sb(ctx, "raw", [P, 4, D])
    front = ExitStack()
    cmask = sb(front, "cmask", [P, P], BF16)
    ident_b = sb(front, "ident_b", [P, P], BF16)
    smask = sb(front, "smask", [P, 2, P], BF16)
    e_head = sb(front, "e_head", [72, H, P], BF16)
    e_row = sb(front, "e_row", [P, PAIRS * 2, P], BF16)
    c_prompt = sb(front, "c_prompt", [72, SEQ], BF16)
    c_past = sb(front, "c_past", [P, 2, KEYS], BF16)
    kgain = sb(front, "kgain", [P, DH])
    qgain = sb(front, "qgain", [P, 1])

    NL = NT * H + LC
    lru = ExitStack()
    wl_hi = sb(lru, "wl_hi", [P, 2, KC, P], F32R)
    wl_lo = sb(lru, "wl_lo", [P, 2, KC, P], F32R)
    l_in = sb(lru, "l_in", [P, NL])
    l_e = sb(lru, "l_e", [P, NL])
    l_s = sb(lru, "l_s", [P, NL])
    l_q = sb(lru, "l_q", [P, NL])
    cl = sb(lru, "cl", [P, KP, DEC_B * H])
    lf_own = sb(lru, "lf_own", [P, DEC_B, H])
    ones_w = sb(lru, "ones_w", [64, 512])
    cc = sb(lru, "cc", [64, KEYS])
    cc_new = sb(lru, "cc_new", [64, DEC_T])
    c_new = sb(lru, "c_new", [64, DEC_T])
    c_mid = sb(lru, "c_mid", [64, KEYS], BF16)
    cp = sb(lru, "cp", [H, SEQ])
    cp_mid = sb(lru, "cp_mid", [H, SEQ], BF16)
    block_of = sb(lru, "block_of", [P, DEC_B])
    xpad = sb(lru, "xpad", [P, 3 + SEQ])
    spad = sb(lru, "spad", [P, DEC_B, 3 + DEC_T])
    pc = sb(lru, "pc", [P, PW])
    gate_w = sb(lru, "gate_w", [P, 2, P])
    l_f = sb(lru, "l_f", [P, NL])
    start = ExitStack()
    x_in = sb(start, "x_in", [P, 3, D])
    ln1_b = sb(start, "ln1_b", [P, D])
    rows = sb(start, "rows", [ROWS, LW])
    wf_raw = sb(start, "wf_raw", [P, KC, H])
    wf_hi = sb(start, "wf_hi", [P, KC, H], F32R)
    wf_lo = sb(start, "wf_lo", [P, KC, H], F32R)
    bf_b = sb(start, "bf_b", [P, H])
    build = sb(start, "build", [P, H * P])
    build2 = sb(start, "build2", [P, P])
    f_rows = sb(start, "f_rows", [H, T_ALL])
    start.close()
    work = ExitStack()
    xc = sb(work, "xc", [P, T_ALL])
    gy = sb(work, "gy", [P, T_ALL])
    tr = sb(work, "tr", [P, T_ALL])
    decay = sb(work, "decay", [P, T_ALL])
    a2 = sb(work, "a2", [P, T_ALL])
    tl = sb(work, "tl", [P, T_ALL])
    ti = sb(work, "ti", [P, T_ALL])
    ah = sb(work, "ah", [P, DEC_B])
    work.close()
    lru.close()
    pair = ExitStack()
    PW3 = 3 * P
    wp_hi = sb(pair, "wp_hi", [P, KC, PW3], F32R)
    wp_lo = sb(pair, "wp_lo", [P, KC, PW3], F32R)
    qt = sb(pair, "qt", [P, T_ALL])
    kt_all = sb(pair, "kt_all", [P, T_ALL])
    vt = sb(pair, "vt", [P, NT, P])
    qk = sb(pair, "qk", [P, 3, 2 * P])
    sqj = sb(pair, "sqj", [P, 2 * P])
    s4 = sb(pair, "s4", [P, 2, 4])
    m4 = sb(pair, "m4", [P, 2, 4])
    rs4 = sb(pair, "rs4", [P, 2, 4])
    probs = sb(pair, "probs", [P, 2, D])
    pts = sb(pair, "pts", [P, 4, 512])
    k_c = sb(pair, "k_c", [P, 2, KP, P])
    v_c = sb(pair, "v_c", [P, 4, KP, P])
    q_blocks = sb(pair, "q_blocks", [P, DEC_B, 2, DEC_T])
    top = sb(pair, "top", [P, 2])
    neg_top = sb(pair, "neg_top", [P, 2])
    den = sb(pair, "den", [P, 16])
    o_tok = sb(pair, "o_tok", [P, 2, P])
    rden = sb(pair, "rden", [P, 2, 2])
    pair.close()
    front.close()
    out = ExitStack()
    wo_hi = sb(out, "wo_hi", [P, KC, D], F32R)
    wo_lo = sb(out, "wo_lo", [P, KC, D], F32R)
    x_e = sb(out, "x_e", [P, 2, KC, P])
    sq = sb(out, "sq", [P, KC, P])
    ssq = sb(out, "ssq", [P, 2, P])
    ln2_b = sb(out, "ln2_b", [P, KC, P])
    ms2 = sb(out, "ms2", [P, 2, 2])
    rs2 = sb(out, "rs2", [P, 2, 2])
    kept = raw[0:36, 3, 0:LW]
    out.close()
    mlp = ExitStack()
    u_hi = sb(mlp, "u_hi", [P, 2, 2, T_ALL], F32R)
    u_lo = sb(mlp, "u_lo", [P, 2, 2, T_ALL], F32R)
    wu_hi = sb(mlp, "wu_hi", [P, 2, KC, P], F32R)
    wu_lo = sb(mlp, "wu_lo", [P, 2, KC, P], F32R)
    wd_hi = sb(mlp, "wd_hi", [P, 2, D], F32R)
    wd_lo = sb(mlp, "wd_lo", [P, 2, D], F32R)
    up = sb(mlp, "up", [P, G, GN])
    mlp.close()
    psum = ctx.enter_context(nc.psum_tensor("psum", [P, 8, 512], F32))

    x_landed = [sem(f"x_landed{i}") for i in range(3)]
    small_in = sem("small_in")
    ln1_in = sem("ln1_in")
    wf_in = sem("wf_in")
    consts_built = sem("consts_built")
    consts_ready = sem("consts_ready")
    x_squared = sem("x_squared")
    x_mean = sem("x_mean")
    x_rstd = sem("x_rstd")
    x_normed = sem("x_normed")
    x_turned = sem("x_turned")
    h_hi_ready = sem("h_hi_ready")
    h_lo_ready = sem("h_lo_ready")
    rows_turned = sem("rows_turned")
    wf_split = sem("wf_split")
    f_done = sem("f_done")
    f_copied = sem("f_copied")
    f_turned = sem("f_turned")
    wf_ready = sem("wf_ready")
    params_copied = sem("params_copied")
    c_read = sem("c_read")
    pair_proj, pair_sq, v_done = sem("pair_proj"), sem("pair_sq"), sem("v_done")
    s4_ready, rs4_ready, qk_ready, qk_turned = sem("s4_ready"), sem("rs4_ready"), sem("qk_ready"), sem("qk_turned")
    q_done, k_done = sem("q_done"), sem("k_done")
    k_out = [sem(f"k_out{i}") for i in range(3)]
    v_out = sem("v_out")
    scores, top_ready, exp_done = sem("scores"), sem("top_ready"), sem("exp_done")
    p_turned, pt_a, pt_b, pv_done = sem("p_turned"), sem("pt_a"), sem("pt_b"), sem("pv_done")
    o_scaled, o_turned, o_done = sem("o_scaled"), sem("o_turned"), sem("o_done")
    q_blocks_ready = sem("q_blocks_ready")
    kc_in = [sem(f"kc_in{i}") for i in range(2)]
    vc_in = [sem(f"vc_in{i}") for i in range(4)]
    kc_turned, kts_a, kts_b = sem("kc_turned"), sem("kts_a"), sem("kts_b")
    s_scores, s_top, s_exp, s_probs = sem("s_scores"), sem("s_top"), sem("s_exp"), sem("s_probs")
    s_turned, s_pta, s_ptb, s_pv, s_out = sem("s_turned"), sem("s_pta"), sem("s_ptb"), sem("s_pv"), sem("s_out")
    ln2_in = sem("ln2_in")
    xe_in = [sem("xe_in0"), sem("xe_in1")]
    mix_sq, mix_ssq, mix_sums, mix_ms, mix_rs = sem("mix_sq"), sem("mix_ssq"), sem("mix_sums"), sem("mix_ms"), sem("mix_rs")
    mix_hi, mix_lo, out_done = sem("mix_hi"), sem("mix_lo"), sem("out_done")
    x1_ready, x1_sq, x1_ms, x1_rs = sem("x1_ready"), sem("x1_sq"), sem("x1_ms"), sem("x1_rs")
    h2_ready, h2_turned, h2_hi, h2_lo = sem("h2_ready"), sem("h2_turned"), sem("h2_hi"), sem("h2_lo")
    up_done, up_read, up_squared, u_ready = sem("up_done"), sem("up_read"), sem("up_squared"), sem("u_ready")
    down_done, y_added = sem("down_done"), sem("y_added")
    SMALL = 1 + 6 + 1 + 1 + 1 + 1 + 2 + KP
    l_abs = sem("l_abs")
    l_exp = sem("l_exp")
    logf_ready = sem("logf_ready")
    gates_free = sem("gates_free")
    raw_in = [sem(f"raw_in{i}") for i in range(4)]
    w_hi = sem("w_hi")
    w_lo = sem("w_lo")
    proj_done = sem("proj_done")
    gate_done = sem("gate_done")
    gw_in = sem("gw_in")
    xr_copied = sem("xr_copied")
    gate_read = sem("gate_read")
    decays_ready = sem("decays_ready")
    xc_ready = sem("xc_ready")
    one_minus_a2 = sem("one_minus_a2")
    root_ready = sem("root_ready")
    mix_ready = sem("mix_ready")
    dve_step = sem("dve_step")
    act_step = sem("act_step")
    stored = sem("stored")
    kept_turned = sem("kept_turned")
    kept_copied = sem("kept_copied")
    c_turned = sem("c_turned")
    c_own_ready = sem("c_own_ready")
    c_ready = sem("c_ready")

    def flat(ap):
        return ap.rearrange("a b d -> (a b) d")

    xp_rows = flat(x_prompt)
    xs_rows = flat(x_sample)

    def x_rows(t):
        return xp_rows[t * P:(t + 1) * P, :] if t < SEQ // P else xs_rows[:, :]

    w_in_k = w_in[0].rearrange("(k p) n -> p k n", p=P)
    V_OUT = 2 * LC + 4 * PAIRS
    V_MLP = V_OUT + KC
    RAW_OUT = 64 + 32 * PAIRS
    RAW_MLP = RAW_OUT + 32
    MLP_STEPS = NFB - 1

    def up_bank(par, m):
        return (6 * par + m) % 4

    DVE_PAIR = 46
    PB = [4, 5, 0]
    QB, KB = [2, 6, 2], [3, 7, 3]
    SB = [4, 6]
    SPAN = 4 * P

    def step_of(s):
        return s // 2, s % 2

    def two_banks(b):
        return psum[:, b:b + 2, :].rearrange("p a n -> p (a n)")

    SPLIT_SUMS = 12
    DVE_LRU = 16
    ACT_LRU = 2

    class Steps:

        def __init__(self, eng, s):
            self.eng, self.s, self.n, self.base = eng, s, 0, 0

        def did(self, ins):
            ins.then_inc(self.s, 1)
            self.n += 1

        def link(self, ins):
            self.did(ins)
            self.eng.wait_ge(self.s, self.base + self.n)

        def enter(self, i, per, before):
            self.base, self.n = before + i * per, 0

        def leave(self, per, before, times):
            assert self.n == per, (self.n, per)
            self.base, self.n = 0, before + per * times

    with nc.allow_non_contiguous_dma(reason="narrow columns of small arrays"), nc.Block() as block:

        @block.sync
        def _(sp):
            n_stored = 0

            def store(dst, src):
                nonlocal n_stored
                sp.dma_start(dst, src).then_inc(stored, 16)
                n_stored += 1

            sp.dma_start(x_in[:, 0, :], x_rows(0)).then_inc(x_landed[0], 16)
            sp.dma_start(ln1_b[:], ln1.to_broadcast([P, D])).then_inc(ln1_in, 16)
            sp.dma_start(x_in[:, 1, :], x_rows(1)).then_inc(x_landed[1], 16)
            sp.dma_start(x_in[:, 2, :], x_rows(2)).then_inc(x_landed[2], 16)
            sp.dma_start(rows[R_CONVW:R_CONVW + CW, :], conv_w[0]).then_inc(small_in, 16)
            for r, a in ((R_CONVB, conv_b), (R_BGA, b_gate_a), (R_BGX, b_gate_x), (R_LAM, lru_lambda),
                         (R_GAO, g_attn_out), (R_GLO, g_lru_out)):
                sp.dma_start(rows[r:r + 1, :], a).then_inc(small_in, 16)
            sp.dma_start(rows[R_H0:R_H0 + DEC_B, :], state_h[0]).then_inc(small_in, 16)
            sp.dma_start(rows[R_CONV:ROWS, :], state_conv[0].rearrange("b j c -> (b j) c")).then_inc(small_in, 16)
            sp.dma_start(bf_b[:], b_f.to_broadcast([P, H])).then_inc(small_in, 16)
            sp.dma_start(kgain[:], k_gain.to_broadcast([P, DH])).then_inc(small_in, 16)
            for hp in range(2):
                sp.dma_start(qgain[hp * DH:(hp + 1) * DH, :], q_gain.rearrange("a d -> d a")).then_inc(small_in, 16)
            sp.dma_start(wf_raw[:], w_in_k[:, :, F_COL:F_COL + H]).then_inc(wf_in, 16)
            for kt in range(KP):
                sp.dma_start(cl[:, kt, :].rearrange("p (b h) -> p b h", b=DEC_B),
                             cache_logf[0, :, kt * P:(kt + 1) * P, :].rearrange("b p h -> p b h")).then_inc(small_in, 16)
            for t in range(3, NT):
                sp.wait_ge(x_turned, 2 * (t - 3) + 2)
                sp.dma_start(x_in[:, t % 3, :], x_rows(t)).then_inc(x_landed[t % 3], 16)

            def lru_weights(c, u):
                sp.dma_start(raw[:, u, :].rearrange("p (k n) -> p k n", k=KC),
                             w_in_k[:, :, bass.ds((XR_COL, YG_COL)[u] + c * P, P)]).then_inc(raw_in[u], 16)

            def gates(c):
                for g, w in enumerate((w_gate_a, w_gate_x)):
                    for b in range(2):
                        sp.dma_start(gate_w[b * DH:(b + 1) * DH, g, b * DH:(b + 1) * DH],
                                     w[0, bass.ds(2 * c + b, 1), :, :].rearrange("a i j -> (a i) j")).then_inc(gw_in, 16)

            lru_weights(0, 0)
            lru_weights(0, 1)
            sp.wait_ge(gates_free, 1)
            gates(0)
            with sp.Fori(0, LC - 1) as c:
                sp.wait_ge(w_lo, 2 * c + 1)
                lru_weights(c + 1, 0)
                sp.wait_ge(w_lo, 2 * c + 2)
                lru_weights(c + 1, 1)
                sp.wait_ge(gate_done, 6 * c + 6)
                gates(c + 1)
            sp.wait_ge(logf_ready, 1)
            for t in range(NT - 1):
                store(logf_prompt[0, 0, t * P:(t + 1) * P, :], l_f[:, t * H:(t + 1) * H])
            store(logf_sample[0].rearrange("b t h -> (b t) h"), l_f[:, (NT - 1) * H:NT * H])

            def pair_weights(p, j):
                for kk in range(2):
                    sp.dma_start(raw[:, j, kk * PW3:(kk + 1) * PW3].rearrange("p (a n) -> p a n", a=3),
                                 w_in[0, (2 * j + kk) * P:(2 * j + kk + 1) * P, 0:3 * AW].rearrange(
                                     "p (a n) -> p a n", a=3)[:, :, bass.ds(p * P, P)]).then_inc(raw_in[j], 16)

            def past_keys(p, b):
                sp.dma_start(k_c[:, b % 2, :, :], cache_k[0, b, :, bass.ds(2 * p, 2), :].rearrange(
                    "(t p) h d -> p t (h d)", p=P)).then_inc(kc_in[b % 2], 16)

            def past_values(p, b):
                sp.dma_start(v_c[:, b % 4, :, :], cache_v[0, b, :, bass.ds(2 * p, 2), :].rearrange(
                    "(t p) h d -> p t (h d)", p=P)).then_inc(vc_in[b % 4], 16)

            for j in range(4):
                if j < 2:
                    sp.wait_ge(w_lo, 2 * LC - 1 + j)
                pair_weights(0, j)
            sp.wait_ge(mix_ready, LC + 1)
            sp.wait_ge(stored, 16 * n_stored)
            for b in range(4):
                past_values(0, b)
            for b in range(2):
                past_keys(0, b)

            def pair_transfers(p, last):
                for t in range(NT):
                    sp.wait_ge(qk_ready, NT * p + t + 1)
                    rows_of = k_prompt[0, 0, t * P:(t + 1) * P] if t < NT - 1 else k_sample[0].rearrange("b t h d -> (b t) h d")
                    sp.dma_start(rows_of[:, bass.ds(2 * p, 2), :],
                                 qk[:, t % 3, P:2 * P].rearrange("p (h d) -> p h d", h=2)).then_inc(k_out[t % 3], 16)
                sp.wait_ge(v_done, NT * p + NT)
                sp.dma_start(v_prompt[0, 0].rearrange("(t p) h d -> p t h d", p=P)[:, :, bass.ds(2 * p, 2), :].rearrange(
                    "p t h d -> p t (h d)"), vt[:, 0:NT - 1, :]).then_inc(v_out, 16)
                sp.dma_start(v_sample[0].rearrange("b t h d -> (b t) h d")[:, bass.ds(2 * p, 2), :],
                             vt[:, NT - 1, :].rearrange("p (h d) -> p h d", h=2)).then_inc(v_out, 16)
                for i in range(3):
                    sp.wait_ge(k_out[i], 48 * p + 48)
                sp.wait_ge(v_out, 32 * p + 32)
                if not last:
                    for j in range(4):
                        sp.wait_ge(w_lo, 2 * LC + 4 * p + j + 1)
                        pair_weights(p + 1, j)
                for b in range(2, DEC_B):
                    sp.wait_ge(kc_turned, DEC_B * p + b - 1)
                    past_keys(p, b)
                sp.wait_ge(s_pv, 2 * p + 1)
                for b in range(4, DEC_B):
                    past_values(p, b)
                if not last:
                    sp.wait_ge(s_pv, 2 * p + 2)
                    for b in range(4):
                        past_values(p + 1, b)
                    for b in range(2):
                        past_keys(p + 1, b)

            with sp.Fori(0, PAIRS - 1) as p:
                pair_transfers(p, False)
            pair_transfers(PAIRS - 1, True)
            for j in range(KC):
                sp.wait_ge(w_lo, V_OUT + j - 3)
                sp.dma_start(raw[:, j % 4, :], w_out[0, j * P:(j + 1) * P, :]).then_inc(raw_in[j % 4], 16)
            sp.wait_ge(s_out, PAIRS + 1)
            sp.dma_start(ln2_b[:].rearrange("p k n -> p (k n)"), ln2.to_broadcast([P, D])).then_inc(ln2_in, 16)

            def load_xe(t):
                sp.dma_start(x_e[:, t % 2, :, :].rearrange("p k n -> p (k n)"), x_rows(t)).then_inc(xe_in[t % 2], 16)

            def up_weights(b, c, slot_free):
                sp.wait_ge(w_lo, slot_free)
                sp.dma_start(raw[:, c, :].rearrange("p (k n) -> p k n", k=KC),
                             w_up[0].rearrange("(k p) n -> p k n", p=P)[:, :, bass.ds(b * FB + c * P, P)]
                             ).then_inc(raw_in[c], 16)

            def down_weights(i, k, slot_free):
                sp.wait_ge(w_lo, slot_free)
                sp.dma_start(raw[:, k, :], w_down[0, bass.ds(i * FB + k * P, P), :]).then_inc(raw_in[k], 16)

            load_xe(0)
            load_xe(1)
            for c in range(2):
                up_weights(0, c, V_MLP + c - 1)
            sp.wait_ge(kept_copied, 1)
            store(h_prompt[0, :, :], kept[0:1, :])
            store(h_sample[0, :, :], kept[1:9, :])
            store(conv_prompt[0, 0, :, :], kept[9:12, :])
            store(conv_sample[0].rearrange("b j c -> (b j) c"), kept[12:36, :])
            for t in range(2, NT):
                sp.wait_ge(h2_turned, 2 * (t - 2) + 2)
                load_xe(t)
            sp.wait_ge(stored, 16 * n_stored)
            for c in range(2):
                up_weights(1, c, V_MLP + 2 + c - 1)
            with sp.Fori(0, MLP_STEPS - 1) as i:
                for k in range(2):
                    down_weights(i, k, V_MLP + 4 * i + 4 + k - 1)
                for c in range(2):
                    up_weights(i + 2, c, V_MLP + 4 * i + 6 + c - 1)
            for k in range(2):
                down_weights(MLP_STEPS - 1, k, V_MLP + 4 * MLP_STEPS + k - 1)
            for k in range(2):
                down_weights(NFB - 1, k, V_MLP + 4 * MLP_STEPS + 2 + k - 1)
            for t in range(NT):
                sp.wait_ge(y_added, 4 + 2 * NT * (NFB - 1) + 2 * t + 2)
                rows_of = y_prompt[0, t * P:(t + 1) * P, :] if t < NT - 1 else y_sample.rearrange("b t d -> (b t) d")
                store(rows_of.rearrange("p (k n) -> p k n", k=KC), mix[:, :, t * P:(t + 1) * P])
            sp.wait_ge(stored, 16 * n_stored)

        @block.gpsimd
        def _(pool):
            n = Steps(pool, consts_built)
            n.link(nc.gpsimd.memset(ident[:], 0.0))
            n.link(nc.gpsimd.affine_select(ident[:], ident[:], [[-1, P]], ALU.not_equal, 1.0, base=0, channel_multiplier=1))
            n.link(nc.gpsimd.memset(neg_half[:], -0.5))
            nc.gpsimd.memset(ones_col[:], 1.0).then_inc(consts_ready, 1)
            for t in range(NT):
                pool.wait_ge(x_mean, t + 1)
                nc.gpsimd.tensor_tensor(x_rs[:, t:t + 1], x_ms[:, t:t + 1], neg_half[:, 0:1], ALU.pow).then_inc(x_rstd, 1)
            nc.gpsimd.memset(gate_w[:], 0.0).then_inc(gates_free, 1)
            n.link(nc.gpsimd.memset(ones_w[:], 1.0))
            n.link(nc.gpsimd.memset(c_prompt[:], 0.0))
            n.link(nc.gpsimd.memset(c_past[:], 0.0))
            n.link(nc.gpsimd.memset(build2[:], 0.0))
            n.link(nc.gpsimd.affine_select(build2[:], build2[:], [[-1, P]], ALU.is_ge, MASKED, base=0, channel_multiplier=1))
            n.link(nc.gpsimd.tensor_copy(cmask[:], build2[:]))
            n.link(nc.gpsimd.tensor_copy(ident_b[:], ident[:]))
            n.link(nc.gpsimd.memset(block_of[:], 1.0))
            n.link(nc.gpsimd.affine_select(block_of[:], block_of[:], [[-DEC_T, DEC_B]], ALU.is_ge, 0.0, base=0,
                                           channel_multiplier=1))
            n.link(nc.gpsimd.affine_select(block_of[:], block_of[:], [[DEC_T, DEC_B]], ALU.is_ge, 0.0,
                                           base=DEC_T - 1, channel_multiplier=-1))
            eh = build[:, :].rearrange("p (h m) -> p h m", h=H)
            n.link(nc.gpsimd.memset(build[:], 0.0))
            for r in range(3):
                n.link(nc.gpsimd.affine_select(eh, eh, [[-1, H], [0, P]], ALU.not_equal, 1.0, base=-32 * r,
                                               channel_multiplier=1))
            n.link(nc.gpsimd.tensor_copy(e_head[:], eh[0:72]))
            er = build[:, :].rearrange("p (a g h q) -> p a g h q", a=PAIRS, g=DEC_B, h=2)
            n.link(nc.gpsimd.memset(build[:], 0.0))
            for r in range(2):
                n.link(nc.gpsimd.affine_select(er, er, [[-2, PAIRS], [-8, DEC_B], [-1, 2], [0, DEC_T]], ALU.not_equal,
                                               1.0, base=-64 * r, channel_multiplier=1))
            n.link(nc.gpsimd.tensor_copy(e_row[:].rearrange("p a m -> p (a m)"), build[:]))
            for g in range(2):
                for hp, fill in enumerate((-(2.0 ** 50), 2.0 ** 50)):
                    v = build[:, hp * P:(hp + 1) * P].rearrange("p (b t) -> p b t", b=DEC_B)
                    n.link(nc.gpsimd.memset(build[:, hp * P:(hp + 1) * P], 0.0))
                    n.link(nc.gpsimd.affine_select(v, v, [[-32, DEC_B], [-1, DEC_T]], ALU.is_ge, fill,
                                                   base=P * g - DEC_T * hp, channel_multiplier=1))
                    n.link(nc.gpsimd.affine_select(v, v, [[32, DEC_B], [0, DEC_T]], ALU.is_ge, fill,
                                                   base=DEC_T * (hp + 1) - 1 - P * g, channel_multiplier=-1))
                n.link(nc.gpsimd.tensor_tensor(build[:, 0:P], build[:, 0:P], build[:, P:2 * P], ALU.mult))
                n.link(nc.gpsimd.tensor_copy(smask[:, g, :], build[:, 0:P]))
            nc.gpsimd.memset(xpad[:, 0:3], 0.0).then_inc(consts_ready, 1)

            def pair_rstd(p):
                for t in range(NT):
                    pool.wait_ge(s4_ready, NT * p + t + 1)
                    nc.gpsimd.tensor_tensor(rs4[:, t % 2, :], m4[:, t % 2, :], neg_half[:], ALU.pow).then_inc(rs4_ready, 1)

            with pool.Fori(0, PAIRS) as p:
                pair_rstd(p)

            def mix_rstd(t):
                pool.wait_ge(mix_ms, t + 1)
                nc.gpsimd.tensor_tensor(rs2[:, t % 2, :], ms2[:, t % 2, :], neg_half[:, 0:2], ALU.pow).then_inc(mix_rs, 1)

            mix_rstd(0)
            mix_rstd(1)
            for t in range(NT):
                if t < NT - 2:
                    mix_rstd(t + 2)
                pool.wait_ge(x1_ms, t + 1)
                nc.gpsimd.tensor_tensor(x_rs[:, t:t + 1], x_ms[:, t:t + 1], neg_half[:, 0:1], ALU.pow).then_inc(x1_rs, 1)

        @block.scalar
        def _(act):
            a = Steps(act, act_step)

            def turn_hi(t):
                for b in range(2):
                    act.wait_ge(x_turned, 2 * t + b + 1)
                    nc.scalar.copy(h_hi[:, 4 * b:4 * b + 4, t * P:(t + 1) * P],
                                   psum[:, 2 * (t % 2) + b, :].rearrange("p (k n) -> p k n", k=4)).then_inc(h_hi_ready, 1)

            for t in range(NT):
                act.wait_ge(x_landed[t % 3], 16 * (t // 3 + 1))
                if t >= 1:
                    act.wait_ge(x_squared, t)
                nc.scalar.activation(mix[:, 0, 0:D], x_in[:, t % 3, :], ACT.Square,
                                     accum_out=x_ss[:, t:t + 1]).then_inc(x_squared, 1)
                if t >= 2:
                    turn_hi(t - 2)
            turn_hi(NT - 2)
            turn_hi(NT - 1)
            act.wait_ge(wf_in, 16)
            nc.scalar.copy(wf_hi[:], wf_raw[:]).then_inc(wf_split, 1)

            def lru_hi(c, u):
                act.wait_ge(raw_in[u], 16 * c + 16)
                nc.scalar.copy(wl_hi[:, u, :, :].rearrange("p k n -> p (k n)"), raw[:, u, :]).then_inc(w_hi, 1)

            lru_hi(0, 0)
            lru_hi(0, 1)
            for g in range(G):
                act.wait_ge(f_done, g + 1)
                nc.scalar.copy(f_rows[:, g * GN:(g + 1) * GN], psum[0:H, 5 + g, 0:GN]).then_inc(f_copied, 1)
            act.wait_ge(l_abs, 1)
            nc.scalar.activation(l_e[:], l_e[:], ACT.Exp, scale=-1.0).then_inc(l_exp, 1)

            def pair_hi(p, j):
                act.wait_ge(raw_in[j], (64 if j < 2 else 0) + 32 * p + 32)
                nc.scalar.copy(wp_hi[:, 2 * j:2 * j + 2, :].rearrange("p k n -> p (k n)"),
                               raw[:, j, 0:2 * PW3]).then_inc(w_hi, 1)

            def chunk(c, last):
                for g in range(G):
                    act.wait_ge(proj_done, 6 * c + g + 1)
                    if g < 2:
                        nc.scalar.copy(xpad[:, 3 + g * GN:3 + (g + 1) * GN], psum[:, g, 0:GN]).then_inc(xr_copied, 1)
                nc.scalar.copy(xpad[:, 3 + 2 * GN:], psum[:, 2, 0:SEQ - 2 * GN]).then_inc(xr_copied, 1)
                nc.scalar.copy(spad[:, :, 3:], psum[:, 2, SEQ - 2 * GN:GN].rearrange(
                    "p (b t) -> p b t", b=DEC_B)).then_inc(xr_copied, 1)
                if not last:
                    lru_hi(c + 1, 0)
                act.wait_ge(mix_ready, c + 1)
                for g in range(G):
                    act.wait_ge(proj_done, 6 * c + 3 + g + 1)
                    nc.scalar.activation(gy[:, g * GN:(g + 1) * GN], psum[:, 3 + g, 0:GN], ACT.Gelu_apprx_tanh)
                if not last:
                    lru_hi(c + 1, 1)
                for m in range(6):
                    act.wait_ge(gate_done, 6 * c + m + 1)
                    dst, g = (tr, ti)[m // 3], m % 3
                    nc.scalar.activation(dst[:, g * GN:(g + 1) * GN], psum[:, 6 + m % 2, 0:GN], ACT.Tanh, scale=0.5,
                                         bias=pc[:, R_HBGA + m // 3:R_HBGA + m // 3 + 1]).then_inc(gate_read, 1)
                act.wait_ge(gate_read, 6 * c + 6)
                if last:
                    act.wait_ge(c_ready, 1)
                    for j in range(4):
                        pair_hi(0, j)
                a.link(nc.scalar.activation(decay[:], tr[:], ACT.Exp, scale=pc[:, R_NSP4:R_NSP4 + 1],
                                            bias=pc[:, R_NSP4:R_NSP4 + 1]))
                a.did(nc.scalar.activation(tl[:], tr[:], ACT.Tanh, scale=pc[:, R_SP4:R_SP4 + 1],
                                           bias=pc[:, R_SP4:R_SP4 + 1]))
                nc.scalar.activation(a2[:], decay[:], ACT.Square).then_inc(decays_ready, 1)
                act.wait_ge(one_minus_a2, c + 1)
                nc.scalar.activation(tr[:], a2[:], ACT.Sqrt, scale=0.25).then_inc(root_ready, 1)

            act.wait_ge(consts_ready, 2)
            before = a.n
            with act.Fori(0, LC - 1) as c:
                a.enter(c, ACT_LRU, before)
                chunk(c, False)
                a.leave(ACT_LRU, before, LC - 1)
            a.enter(LC - 1, ACT_LRU, before)
            chunk(LC - 1, True)
            a.leave(ACT_LRU, before, LC)
            act.wait_ge(mix_ready, LC + 1)
            nc.scalar.copy(den[:, 0:2], ident[:, 0:2]).then_inc(s_out, 1)

            def pair_act(p, last):
                def q_out(g):
                    n = SPAN if g < 2 else P
                    act.wait_ge(qk_turned, NT * p + min(4 * g + 4, NT))
                    nc.scalar.activation(qt[:, g * SPAN:g * SPAN + n], psum[:, QB[g], 0:n], ACT.Copy,
                                         scale=qgain[:, 0:1]).then_inc(q_done, 1)

                for t in range(NT):
                    act.wait_ge(pair_proj, NT * p + t + 1)
                    nc.scalar.copy(vt[:, t, :], psum[:, PB[t % 3], 2 * P:PW3]).then_inc(v_done, 1)
                    if t >= 1:
                        act.wait_ge(s4_ready, NT * p + t)
                    nc.scalar.activation(sqj[:], psum[:, PB[t % 3], 0:2 * P], ACT.Square).then_inc(pair_sq, 1)
                    if t == 6:
                        q_out(0)
                q_out(1)
                q_out(2)

                def exp(s):
                    nk = step_of(s)[0] + 1
                    act.wait_ge(top_ready, 16 * p + s + 1)
                    nc.scalar.activation(probs[:, s % 2, 0:nk * P], two_banks(SB[s % 2])[:, 0:nk * P], ACT.Exp,
                                         bias=neg_top[:, s % 2:s % 2 + 1],
                                         accum_out=den[:, s:s + 1]).then_inc(exp_done, 1)

                def turned_a(s):
                    n = min(step_of(s)[0] + 1, 4)
                    act.wait_ge(p_turned, 16 * p + s + 1)
                    nc.scalar.copy(pts[:, 2 * (s % 2), 0:n * P], psum[:, 2, 0:n * P]).then_inc(pt_a, 1)

                def heads_out(t):
                    act.wait_ge(o_turned, 8 * p + t + 1)
                    nc.scalar.copy(mix[:, bass.ds(p, 1), t * P:(t + 1) * P].rearrange("p a n -> p (a n)"),
                                   psum[:, t % 2, P:2 * P]).then_inc(o_done, 1)

                exp(0)
                for s in range(16):
                    turned_a(s)
                    if s < 15:
                        exp(s + 1)
                    if s >= 4 and s % 2 == 0:
                        heads_out((s - 4) // 2)
                    if not last and s in (3, 5, 7, 9):
                        pair_hi(p + 1, (s - 3) // 2)
                heads_out(6)
                heads_out(7)
                def past_turned(g):
                    act.wait_ge(s_turned, 2 * p + g + 1)
                    nc.scalar.copy(pts[:, 2 * g, :], psum[:, 2, :]).then_inc(s_pta, 1)

                for b in range(0, DEC_B, 2):
                    act.wait_ge(kc_turned, DEC_B * p + b + 1)
                    nc.scalar.copy(pts[:, 2, :], psum[:, 2, :]).then_inc(kts_a, 1)
                    if b >= 4:
                        g = b // 2 - 2
                        if g == 1:
                            past_turned(0)
                        act.wait_ge(s_top, 2 * p + g + 1)
                        nc.scalar.activation(probs[:, g, 0:KEYS], two_banks(SB[g])[:, 0:KEYS], ACT.Exp,
                                             bias=neg_top[:, g:g + 1], accum_out=den[:, g:g + 1]).then_inc(s_exp, 1)
                for g in range(2):
                    if g == 1:
                        past_turned(1)
                    act.wait_ge(s_pv, 2 * p + g + 1)
                    for hp in range(2):
                        last_out = nc.scalar.copy(
                            mix[hp * DH:(hp + 1) * DH, bass.ds(p, 1), SEQ + g * DH:SEQ + (g + 1) * DH].rearrange(
                                "p a (b q) -> p (a b) q", b=4),
                            psum[hp * DH:(hp + 1) * DH, g, 0:P].rearrange("p (b h q) -> p b h q", b=4, h=2)[:, :, hp, :])
                last_out.then_inc(s_out, 1)

            with act.Fori(0, PAIRS - 1) as p:
                pair_act(p, False)
            pair_act(PAIRS - 1, True)

            def tile(t):
                return slice(t * P, (t + 1) * P)

            def mix_act(t):
                if t == 0:
                    act.wait_ge(s_out, PAIRS + 1)
                else:
                    act.wait_ge(mix_ssq, t)
                nc.scalar.activation(sq[:], mix[:, :, tile(t)], ACT.Square).then_inc(mix_sq, 1)
                nc.scalar.copy(h_hi[:, :, tile(t)], mix[:, :, tile(t)]).then_inc(mix_hi, 1)

            act.wait_ge(s_pv, 2 * PAIRS)
            for j in range(KC):
                r = R_GAO if j < LC else R_GLO
                act.wait_ge(raw_in[j % 4], RAW_OUT - (0 if j % 4 < 2 else 64) + 16 * (j // 4) + 16)
                nc.scalar.activation(wo_hi[:, j, :], raw[:, j % 4, :], ACT.Copy,
                                     scale=param[:, j % LC, r:r + 1]).then_inc(w_hi, 1)
                if j in (1, 3):
                    mix_act(j // 2)
            def up_hi(b, c, landed, freed):
                act.wait_ge(raw_in[c], landed)
                act.wait_ge(up_done, freed)
                nc.scalar.copy(wu_hi[:, c, :, :].rearrange("p k n -> p (k n)"), raw[:, c, :]).then_inc(w_hi, 1)

            for t in range(NT):
                if t < NT - 2:
                    mix_act(t + 2)
                elif t == NT - 1:
                    act.wait_ge(out_done, 2 * NT)
                    for c in range(2):
                        act.wait_ge(raw_in[c], RAW_MLP + 16)
                        nc.scalar.copy(wu_hi[:, c, :, :].rearrange("p k n -> p (k n)"), raw[:, c, :]).then_inc(w_hi, 1)
                if t == 0:
                    act.wait_ge(kept_turned, 1)
                    act.wait_ge(w_lo, V_MLP)
                    nc.scalar.copy(kept, psum[0:36, 7, :]).then_inc(kept_copied, 1)
                act.wait_ge(x1_ready, 2 * t + 2)
                nc.scalar.activation(x_e[:, t % 2, :, :], mix[:, :, tile(t)], ACT.Square,
                                     accum_out=x_ss[:, t:t + 1]).then_inc(x1_sq, 1)
                for u in ([t - 1] if t < NT - 1 else [t - 1, t]) if t else []:
                    for b in range(2):
                        act.wait_ge(h2_turned, 2 * u + b + 1)
                        nc.scalar.copy(h_hi[:, 4 * b:4 * b + 4, tile(u)],
                                       psum[:, 4 + b, :].rearrange("p (k n) -> p k n", k=4)).then_inc(h2_hi, 1)

            def relu_squared(b, par, m, first=False):
                n = 6 * b + m
                act.wait_ge(up_done, n + 1)
                if m >= 3:
                    act.wait_ge(u_ready, n - 2)
                elif not first:
                    act.wait_ge(u_ready, 6 * b)
                nc.scalar.activation(up[:, m % 3, :], psum[:, up_bank(par, m), 0:GN], ACT.Relu).then_inc(up_read, 1)
                act.wait_ge(up_read, n + 1)
                nc.scalar.activation(up[:, m % 3, :], up[:, m % 3, :], ACT.Square).then_inc(up_squared, 1)

            def down_hi(i, k, landed):
                act.wait_ge(raw_in[k], landed)
                nc.scalar.copy(wd_hi[:, k, :], raw[:, k, :]).then_inc(w_hi, 1)

            for m in range(6):
                relu_squared(0, 0, m, True)
                if m in (2, 5):
                    up_hi(1, m // 3, RAW_MLP + 32, 3 * (m // 3) + 3)

            def mlp_act(i, par, more):
                act.wait_ge(up_done, 6 * i + 7)
                for k in range(2):
                    down_hi(i, k, RAW_MLP + 32 * i + 48)
                for m in range(6):
                    relu_squared(i + 1, par, m)
                    if more and m in (2, 5):
                        up_hi(i + 2, m // 3, RAW_MLP + 32 * i + 64, 6 * i + 6 + m + 1)

            with act.Fori(0, (MLP_STEPS - 1) // 2) as j:
                for o in range(2):
                    mlp_act(2 * j + o, (o + 1) % 2, True)
            mlp_act(MLP_STEPS - 1, MLP_STEPS % 2, False)
            act.wait_ge(down_done, 2 * NT * MLP_STEPS)
            for k in range(2):
                down_hi(NFB - 1, k, RAW_MLP + 16 * 32)


        @block.vector
        def _(dve):
            d = Steps(dve, dve_step)

            def h2_of(dve, t):
                dve.wait_ge(x1_rs, t + 1)
                nc.vector.scalar_tensor_tensor(x_e[:, t % 2, :, :], mix[:, :, t * P:(t + 1) * P], x_rs[:, t:t + 1],
                                               ln2_b[:], ALU.mult, ALU.mult).then_inc(h2_ready, 1)

            nc.vector.memset(ah[:], 0.0).then_inc(mix_ready, 1)

            def x_mean_of(t):
                dve.wait_ge(x_squared, t + 1)
                nc.vector.tensor_scalar(x_ms[:, t:t + 1], x_ss[:, t:t + 1], 1.0 / D, EPS, ALU.mult, ALU.add).then_inc(x_mean, 1)

            def x_norm(t):
                dve.wait_ge(x_rstd, t + 1)
                nc.vector.scalar_tensor_tensor(x_in[:, t % 3, :], x_in[:, t % 3, :], x_rs[:, t:t + 1], ln1_b[:],
                                               ALU.mult, ALU.mult).then_inc(x_normed, 1)

            def turn_lo(t):
                for b in range(2):
                    dve.wait_ge(h_hi_ready, 2 * t + b + 1)
                    at = (slice(None), slice(4 * b, 4 * b + 4), slice(t * P, (t + 1) * P))
                    nc.vector.tensor_tensor(h_lo[at], psum[:, 2 * (t % 2) + b, :].rearrange("p (k n) -> p k n", k=4),
                                            h_hi[at].bitcast(F32), ALU.subtract).then_inc(h_lo_ready, 1)

            dve.wait_ge(ln1_in, 16)
            for t in range(NT):
                x_mean_of(t)
                if t == 5:
                    dve.wait_ge(small_in, 16 * SMALL)
                    dve.wait_ge(rows_turned, 1)
                    nc.vector.tensor_copy(param[:, :, 0:ROWS], psum[:, 4, 0:LC * ROWS].rearrange(
                        "p (c r) -> p c r", c=LC)).then_inc(params_copied, 1)
                if t >= 2:
                    turn_lo(t - 2)
                x_norm(t)
            turn_lo(NT - 2)
            turn_lo(NT - 1)
            dve.wait_ge(wf_split, 1)
            nc.vector.tensor_tensor(wf_lo[:], wf_raw[:], wf_hi[:].bitcast(F32), ALU.subtract).then_inc(wf_ready, 1)

            def lru_lo(c, u):
                dve.wait_ge(w_hi, 2 * c + u + 1)
                nc.vector.tensor_tensor(wl_lo[:, u, :, :].rearrange("p k n -> p (k n)"), raw[:, u, :],
                                        wl_hi[:, u, :, :].rearrange("p k n -> p (k n)").bitcast(F32),
                                        ALU.subtract).then_inc(w_lo, 1)

            lru_lo(0, 0)
            lru_lo(0, 1)
            dve.wait_ge(f_turned, 1)
            d.did(nc.vector.tensor_tensor(l_in[:, 0:NT * H].rearrange("p (t h) -> p t h", h=H),
                                          psum[:, 4, 256:256 + NT * H].rearrange("p (t h) -> p t h", h=H),
                                          bf_b[:, None, :].to_broadcast([P, NT, H]), ALU.add))
            d.link(nc.vector.tensor_copy(l_in[:, NT * H:NL], param[:, :, R_LAM]))
            nc.vector.scalar_tensor_tensor(l_e[:], l_in[:], -1.0, l_in[:], ALU.mult, ALU.max).then_inc(l_abs, 1)
            dve.wait_ge(l_exp, 1)
            d.link(nc.vector.tensor_scalar(l_s[:], l_e[:], 2.0, None, ALU.add))
            d.link(nc.vector.reciprocal(l_q[:], l_s[:]))
            d.link(nc.vector.tensor_tensor(l_s[:], l_e[:], l_q[:], ALU.mult))
            d.link(nc.vector.tensor_tensor(l_q[:], l_s[:], l_s[:], ALU.mult))
            d.link(nc.vector.tensor_scalar(l_f[:], l_q[:], 1.0 / 15, None, ALU.mult))
            for odd in (13, 11, 9, 7, 5, 3):
                d.link(nc.vector.scalar_tensor_tensor(l_f[:], l_f[:], 1.0 / odd, l_q[:], ALU.add, ALU.mult))
            d.link(nc.vector.scalar_tensor_tensor(l_e[:], l_f[:], 1.0, l_s[:], ALU.add, ALU.mult))
            d.link(nc.vector.tensor_scalar(l_in[:], l_in[:], 0.0, None, ALU.min))
            nc.vector.scalar_tensor_tensor(l_f[:], l_e[:], -2.0, l_in[:], ALU.mult, ALU.add).then_inc(logf_ready, 1)
            dve.wait_ge(logf_ready, 1)
            nc.vector.tensor_scalar(param[:, :, R_SP4], l_f[:, NT * H:NL], -4.0, None, ALU.mult)
            nc.vector.tensor_scalar(param[:, :, R_NSP4], l_f[:, NT * H:NL], 4.0, None, ALU.mult)
            d.link(nc.vector.tensor_scalar(param[:, :, R_HBGA:R_HBGX + 1], param[:, :, R_BGA:R_BGX + 1], 0.5, None,
                                           ALU.mult))

            def pair_lo(p, j):
                dve.wait_ge(w_hi, 2 * LC + 4 * p + j + 1)
                nc.vector.tensor_tensor(wp_lo[:, 2 * j:2 * j + 2, :].rearrange("p k n -> p (k n)"), raw[:, j, 0:2 * PW3],
                                        wp_hi[:, 2 * j:2 * j + 2, :].rearrange("p k n -> p (k n)").bitcast(F32),
                                        ALU.subtract).then_inc(w_lo, 1)

            starts = slice(SEQ, T_ALL, DEC_T)

            def split_sums():
                for c_all, mid, hi_at, mid_at, lo_at in (
                        (cc, c_mid, c_past[0:64, 0, :], c_past[64:P, 0, :], c_past[0:64, 1, :]),
                        (cp, cp_mid, c_prompt[0:H, :], c_prompt[32:32 + H, :], c_prompt[64:64 + H, :])):
                    d.link(nc.vector.tensor_scalar(hi_at, c_all[:], -1.0, None, ALU.mult))
                    d.link(nc.vector.scalar_tensor_tensor(c_all[:], c_all[:], -1.0, hi_at, ALU.mult, ALU.subtract))
                    d.link(nc.vector.tensor_copy(mid[:], c_all[:]))
                    d.did(nc.vector.tensor_copy(mid_at, mid[:]))
                    d.link(nc.vector.tensor_tensor(c_all[:], c_all[:], mid[:], ALU.subtract))
                    d.link(nc.vector.tensor_copy(lo_at, c_all[:]))
                nc.vector.memset(c_new[:, 0:1], 0.0).then_inc(c_ready, 1)

            def chunk(c, last):
                d.link(nc.vector.tensor_copy(pc[:], param[:, bass.ds(c, 1), :]))
                d.link(nc.vector.tensor_copy(spad[:, :, 0:3], pc[:, R_CONV:ROWS].rearrange("p (b j) -> p b j", b=DEC_B)))
                dve.wait_ge(xr_copied, 4 * c + 4)
                xcs = xc[:, SEQ:].rearrange("p (b t) -> p b t", b=DEC_B)
                d.did(nc.vector.tensor_scalar(xc[:, 0:SEQ], xpad[:, 3:], pc[:, 3:4], pc[:, R_CONVB:R_CONVB + 1],
                                              ALU.mult, ALU.add))
                d.link(nc.vector.tensor_scalar(xcs, spad[:, :, 3:], pc[:, 3:4], pc[:, R_CONVB:R_CONVB + 1],
                                               ALU.mult, ALU.add))
                for j in (2, 1, 0):
                    d.did(nc.vector.scalar_tensor_tensor(xc[:, 0:SEQ], xpad[:, j:j + SEQ], pc[:, j:j + 1], xc[:, 0:SEQ],
                                                         ALU.mult, ALU.add))
                    d.link(nc.vector.scalar_tensor_tensor(xcs, spad[:, :, j:j + DEC_T], pc[:, j:j + 1], xcs,
                                                          ALU.mult, ALU.add))
                nc.vector.tensor_copy(h_keep[:, bass.ds(c, 1), 9:12], xpad[:, None, SEQ:SEQ + 3])
                nc.vector.tensor_copy(h_keep[:, bass.ds(c, 1), 12:36].rearrange("p a (b j) -> p (a b) j", b=DEC_B),
                                      spad[:, :, DEC_T:]).then_inc(xc_ready, 1)
                if not last:
                    lru_lo(c + 1, 0)
                    lru_lo(c + 1, 1)
                else:
                    split_sums()
                    for j in range(4):
                        pair_lo(0, j)
                dve.wait_ge(decays_ready, c + 1)
                nc.vector.scalar_tensor_tensor(a2[:], a2[:], 1.0, tl[:], ALU.add, ALU.mult).then_inc(one_minus_a2, 1)
                d.did(nc.vector.scalar_tensor_tensor(ti[:], ti[:], 1.0, xc[:], ALU.add, ALU.mult))
                d.link(nc.vector.tensor_tensor(ah[:], decay[:, starts], pc[:, R_H0:R_H0 + DEC_B], ALU.mult))
                dve.wait_ge(root_ready, c + 1)
                d.link(nc.vector.tensor_tensor(ti[:], ti[:], tr[:], ALU.mult))
                d.did(nc.vector.tensor_tensor(ti[:, starts], ti[:, starts], ah[:], ALU.add))
                d.link(nc.vector.memset(decay[:, starts], 0.0))
                d.link(nc.vector.tensor_tensor_scan(tl[:], decay[:], ti[:], 0.0, ALU.mult, ALU.add))
                nc.vector.tensor_copy(h_keep[:, bass.ds(c, 1), 0:1], tl[:, None, SEQ - 1:SEQ])
                nc.vector.tensor_copy(h_keep[:, bass.ds(c, 1), 1:9], tl[:, None, SEQ + DEC_T - 1:T_ALL:DEC_T])
                nc.vector.tensor_tensor(mix[:, bass.ds(c + LC, 1), :].rearrange("p a n -> p (a n)"), gy[:], tl[:],
                                        ALU.mult).then_inc(mix_ready, 1)

            dve.wait_ge(consts_ready, 2)
            nc.vector.tensor_tensor(lf_own[:], l_f[:, None, (NT - 1) * H:NT * H].to_broadcast([P, DEC_B, H]),
                                    block_of[:, :, None].to_broadcast([P, DEC_B, H]), ALU.mult).then_inc(c_own_ready, 1)
            before = d.n
            with dve.Fori(0, LC - 1) as c:
                d.enter(c, DVE_LRU, before)
                chunk(c, False)
                d.leave(DVE_LRU, before, LC - 1)
            dve.wait_ge(c_turned, 1)
            d.link(nc.vector.tensor_tensor_scan(cp[:, 0:512], ones_w[0:H, :], psum[0:H, 3, :], 0.0, ALU.mult, ALU.add))
            d.did(nc.vector.tensor_tensor_scan(cp[:, 512:], ones_w[0:H, :], psum[0:H, 4, :], cp[:, 511:512],
                                               ALU.mult, ALU.add))
            d.did(nc.vector.tensor_tensor_scan(cc[:, 0:PAST], ones_w[:], psum[0:64, 5, :], 0.0, ALU.mult, ALU.add))
            dve.wait_ge(c_turned, 2)
            d.link(nc.vector.reduce_sum(c_new[:], psum[0:64, 6, 0:P].rearrange("p (b t) -> p t b", b=DEC_B), AX_X))
            d.link(nc.vector.tensor_tensor_scan(cc_new[:], ones_w[:, 0:DEC_T], c_new[:], cc[:, PAST - 1:PAST],
                                                ALU.mult, ALU.add))
            nc.vector.tensor_copy(cc[:, PAST:].rearrange("p (b t) -> p b t", b=DEC_B),
                                  cc_new[:, None, :].to_broadcast([64, DEC_B, DEC_T])).then_inc(c_read, 1)
            dve.wait_ge(c_read, 1)
            extra = d.n - before - DVE_LRU * (LC - 1)
            d.enter(LC - 1, DVE_LRU, before + extra)
            chunk(LC - 1, True)
            d.leave(DVE_LRU + SPLIT_SUMS, before + extra - SPLIT_SUMS * (LC - 1), LC)
            nc.vector.tensor_scalar(qgain[:], qgain[:], DH ** -0.5, None, ALU.mult)
            d.link(nc.vector.memset(q_blocks[:], 0.0))

            def pair_dve(p, last):
                def mean(t):
                    dve.wait_ge(pair_sq, NT * p + t + 1)
                    d.link(nc.vector.reduce_sum(s4[:, t % 2, :], sqj[:].rearrange("p (a d) -> p a d", d=DH), AX_X))
                    nc.vector.tensor_scalar(m4[:, t % 2, :], s4[:, t % 2, :], 1.0 / DH, EPS, ALU.mult,
                                            ALU.add).then_inc(s4_ready, 1)

                def norm(t):
                    dve.wait_ge(rs4_ready, NT * p + t + 1)
                    if t >= 3:
                        dve.wait_ge(qk_turned, NT * p + t - 2)
                        dve.wait_ge(k_out[t % 3], 48 * p + 16 * (t // 3))
                    v = qk[:, t % 3, :].rearrange("p (a d) -> p a d", d=DH)
                    d.link(nc.vector.tensor_tensor(v, psum[:, PB[t % 3], 0:2 * P].rearrange("p (a d) -> p a d", d=DH),
                                                   rs4[:, t % 2, :, None].to_broadcast([P, 4, DH]), ALU.mult))
                    nc.vector.tensor_tensor(v[:, 2:4, :], v[:, 2:4, :], kgain[:, None, :].to_broadcast([P, 2, DH]),
                                            ALU.mult).then_inc(qk_ready, 1)

                def k_turn_out(g):
                    n = SPAN if g < 2 else P
                    dve.wait_ge(qk_turned, NT * p + min(4 * g + 4, NT))
                    nc.vector.tensor_copy(kt_all[:, g * SPAN:g * SPAN + n], psum[:, KB[g], 0:n]).then_inc(k_done, 1)

                mean(0)
                for t in range(NT):
                    if t < NT - 1:
                        mean(t + 1)
                    norm(t)
                    if t == 6:
                        k_turn_out(0)
                k_turn_out(1)

                def top_of(s):
                    nk = step_of(s)[0] + 1
                    dve.wait_ge(scores, 16 * p + s + 1)
                    d.link(nc.vector.reduce_max(top[:, s % 2:s % 2 + 1], two_banks(SB[s % 2])[:, 0:nk * P], AX_X))
                    nc.vector.tensor_scalar(neg_top[:, s % 2:s % 2 + 1], top[:, s % 2:s % 2 + 1], -1.0, None,
                                            ALU.mult).then_inc(top_ready, 1)

                def turned_b(s):
                    n = step_of(s)[0] + 1 - 4
                    if n > 0:
                        dve.wait_ge(p_turned, 16 * p + s + 1)
                        nc.vector.tensor_copy(pts[:, 2 * (s % 2) + 1, 0:n * P], psum[:, 3, 0:n * P]).then_inc(pt_b, 1)

                def share(t):
                    dve.wait_ge(exp_done, 16 * p + 2 * t + 2)
                    d.link(nc.vector.reciprocal(rden[:, t % 2, :], den[:, 2 * t:2 * t + 2]))
                    dve.wait_ge(pv_done, 16 * p + 2 * t + 2)
                    nc.vector.tensor_tensor(o_tok[:, t % 2, :].rearrange("p (h d) -> p h d", h=2),
                                            psum[:, t % 2, 0:P].rearrange("p (h d) -> p h d", h=2),
                                            rden[:, t % 2, :, None].to_broadcast([P, 2, DH]), ALU.mult).then_inc(o_scaled, 1)

                top_of(0)
                k_turn_out(2)
                for s in range(16):
                    if s < 15:
                        top_of(s + 1)
                    turned_b(s)
                    if s == 1:
                        for hp in range(2):
                            r = slice(hp * DH, (hp + 1) * DH)
                            dve.wait_ge(q_done, 3 * p + 3)
                            nc.vector.tensor_copy(q_blocks[r, :, hp, :], qt[r, SEQ:].rearrange("p (b q) -> p b q", b=DEC_B)
                                                  ).then_inc(q_blocks_ready, 1)
                    if s >= 2 and s % 2 == 0:
                        share(s // 2 - 1)
                    if not last and s in (4, 6, 8, 10):
                        pair_lo(p + 1, (s - 4) // 2)
                share(7)

                def new_turned(g):
                    dve.wait_ge(s_turned, 2 * p + g + 1)
                    nc.vector.tensor_copy(pts[:, 2 * g + 1, 0:P], psum[:, 3, 0:P]).then_inc(s_ptb, 1)

                for b in range(1, DEC_B, 2):
                    dve.wait_ge(kc_turned, DEC_B * p + b + 1)
                    nc.vector.tensor_copy(pts[:, 3, :], psum[:, 3, :]).then_inc(kts_b, 1)
                    if b in (3, 7):
                        g = b // 4
                        dve.wait_ge(s_scores, 2 * p + g + 1)
                        d.link(nc.vector.reduce_max(top[:, g:g + 1], two_banks(SB[g])[:, 0:KEYS], AX_X))
                        nc.vector.tensor_scalar(neg_top[:, g:g + 1], top[:, g:g + 1], -1.0, None,
                                                ALU.mult).then_inc(s_top, 1)
                    if b == 7:
                        new_turned(0)
                    if b in (5, 7):
                        g = b // 7
                        dve.wait_ge(s_exp, 2 * p + g + 1)
                        d.link(nc.vector.reciprocal(rden[:, 0, g:g + 1], den[:, g:g + 1]))
                        nc.vector.tensor_scalar(probs[:, g, 0:KEYS], probs[:, g, 0:KEYS], rden[:, 0, g:g + 1], None,
                                                ALU.mult).then_inc(s_probs, 1)
                new_turned(1)

            before = d.n
            with dve.Fori(0, PAIRS - 1) as p:
                d.enter(p, DVE_PAIR, before)
                pair_dve(p, False)
                d.leave(DVE_PAIR, before, PAIRS - 1)
            d.enter(PAIRS - 1, DVE_PAIR, before)
            pair_dve(PAIRS - 1, True)
            d.leave(DVE_PAIR, before, PAIRS)

            def tile(t):
                return slice(t * P, (t + 1) * P)

            def mix_squares(t):
                dve.wait_ge(mix_sq, t + 1)
                if t >= 1:
                    dve.wait_ge(mix_sums, t)
                nc.vector.reduce_sum(ssq[:], sq[:].rearrange("p (a k) n -> p a n k", a=2), AX_X).then_inc(mix_ssq, 1)

            def mix_mean(t):
                dve.wait_ge(mix_sums, t + 1)
                nc.vector.tensor_scalar(ms2[:, t % 2, :], psum[:, 6, 0:2], 1.0 / LW, EPS, ALU.mult, ALU.add).then_inc(mix_ms, 1)

            def mix_lo_of(t):
                dve.wait_ge(mix_hi, t + 1)
                nc.vector.tensor_tensor(h_lo[:, :, tile(t)], mix[:, :, tile(t)], h_hi[:, :, tile(t)].bitcast(F32),
                                        ALU.subtract).then_inc(mix_lo, 1)

            for j in range(KC):
                r = R_GAO if j < LC else R_GLO
                dve.wait_ge(w_hi, V_OUT + j + 1)
                nc.vector.scalar_tensor_tensor(wo_lo[:, j, :], raw[:, j % 4, :], param[:, j % LC, r:r + 1],
                                               wo_hi[:, j, :].bitcast(F32), ALU.mult, ALU.subtract).then_inc(w_lo, 1)
                if j in (1, 3):
                    mix_squares(j // 2)
                    mix_mean(j // 2)
                    mix_lo_of(j // 2)
            dve.wait_ge(ln2_in, 16)
            for t in range(NT):
                if t < NT - 2:
                    mix_squares(t + 2)
                    mix_lo_of(t + 2)
                elif t == NT - 1:
                    for c in range(2):
                        dve.wait_ge(w_hi, V_MLP + c + 1)
                        nc.vector.tensor_tensor(wu_lo[:, c, :, :].rearrange("p k n -> p (k n)"), raw[:, c, :],
                                                wu_hi[:, c, :, :].rearrange("p k n -> p (k n)").bitcast(F32),
                                                ALU.subtract).then_inc(w_lo, 1)
                dve.wait_ge(xe_in[t % 2], 16 * (t // 2) + 16)
                dve.wait_ge(mix_rs, t + 1)
                for half in range(2):
                    dve.wait_ge(out_done, 2 * t + half + 1)
                    at = mix[:, 4 * half:4 * half + 4, tile(t)]
                    if half == 0:
                        dve.wait_ge(mix_lo, t + 1)
                    d.link(nc.vector.scalar_tensor_tensor(
                        at, psum[:, 2 * half, :].rearrange("p (k n) -> p k n", n=P), rs2[:, t % 2, 0:1],
                        x_e[:, t % 2, 4 * half:4 * half + 4, :], ALU.mult, ALU.add))
                    last = nc.vector.scalar_tensor_tensor(
                        at, psum[:, 2 * half + 1, :].rearrange("p (k n) -> p k n", n=P), rs2[:, t % 2, 1:2], at,
                        ALU.mult, ALU.add)
                    last.then_inc(x1_ready, 1)
                if t < NT - 2:
                    mix_mean(t + 2)
                dve.wait_ge(x1_sq, t + 1)
                nc.vector.tensor_scalar(x_ms[:, t:t + 1], x_ss[:, t:t + 1], 1.0 / D, EPS, ALU.mult, ALU.add).then_inc(x1_ms, 1)
                for u in ([t - 1] if t else []) + ([t] if t == NT - 1 else []):
                    if u == t:
                        h2_of(dve, t)
                    for b in range(2):
                        dve.wait_ge(h2_hi, 2 * u + b + 1)
                        at = (slice(None), slice(4 * b, 4 * b + 4), tile(u))
                        nc.vector.tensor_tensor(h_lo[at], psum[:, 4 + b, :].rearrange("p (k n) -> p k n", k=4),
                                                h_hi[at].bitcast(F32), ALU.subtract).then_inc(h2_lo, 1)
                if t < NT - 1:
                    h2_of(dve, t)

            for bank in range(4):
                nc.vector.tensor_copy(x_ms[:, 0:1], x_ms[:, 1:2]).then_inc(y_added, 1)
                dve.wait_ge(y_added, bank + 1)

            def up_lo(c, unit):
                dve.wait_ge(w_hi, unit + 1)
                nc.vector.tensor_tensor(wu_lo[:, c, :, :].rearrange("p k n -> p (k n)"), raw[:, c, :],
                                        wu_hi[:, c, :, :].rearrange("p k n -> p (k n)").bitcast(F32),
                                        ALU.subtract).then_inc(w_lo, 1)

            def down_lo(k, unit):
                dve.wait_ge(w_hi, unit + 1)
                nc.vector.tensor_tensor(wd_lo[:, k, :], raw[:, k, :], wd_hi[:, k, :].bitcast(F32),
                                        ALU.subtract).then_inc(w_lo, 1)

            def split_u(b, par, m):
                dve.wait_ge(up_squared, 6 * b + m + 1)
                at = (slice(None), par, m // 3, slice((m % 3) * GN, (m % 3 + 1) * GN))
                d.link(nc.vector.tensor_copy(u_hi[at], up[:, m % 3, :]))
                nc.vector.tensor_tensor(u_lo[at], up[:, m % 3, :], u_hi[at].bitcast(F32), ALU.subtract).then_inc(u_ready, 1)

            def add_y(i):
                for t in range(NT):
                    for half in range(2):
                        dve.wait_ge(down_done, 2 * NT * i + 2 * t + half + 1)
                        at = mix[:, 4 * half:4 * half + 4, tile(t)]
                        nc.vector.tensor_tensor(at, psum[:, 4 + 2 * (t % 2) + half, :].rearrange("p (k n) -> p k n", n=P), at,
                                                ALU.add).then_inc(y_added, 1)

            for m in range(6):
                split_u(0, 0, m)
                if m in (2, 5):
                    up_lo(m // 3, V_MLP + 2 + m // 3)

            def mlp_dve(i, par, more):
                for k in range(2):
                    down_lo(k, V_MLP + 4 * i + 4 + k)
                for m in range(6):
                    split_u(i + 1, par, m)
                    if more and m in (2, 5):
                        up_lo(m // 3, V_MLP + 4 * i + 6 + m // 3)
                add_y(i)

            before = d.n
            with dve.Fori(0, (MLP_STEPS - 1) // 2) as j:
                d.enter(j, 12, before)
                for o in range(2):
                    mlp_dve(2 * j + o, (o + 1) % 2, True)
                d.leave(12, before, (MLP_STEPS - 1) // 2)
            mlp_dve(MLP_STEPS - 1, MLP_STEPS % 2, False)
            for k in range(2):
                down_lo(k, V_MLP + 4 * MLP_STEPS + 2 + k)
            add_y(NFB - 1)

        @block.tensor
        def _(pe):
            def split_product(out, hi, lo, r_hi, r_lo, n, first=True, end=True):
                for k in range(n):
                    nc.tensor.matmul(out, hi(k), r_hi(k), start=first and k == 0, stop=False)
                    nc.tensor.matmul(out, hi(k), r_lo(k), start=False, stop=False)
                    last = nc.tensor.matmul(out, lo(k), r_hi(k), start=False, stop=end and k == n - 1)
                return last

            pe.wait_ge(consts_ready, 1)

            def turn(t):
                pe.wait_ge(x_normed, t + 1)
                if t >= 2:
                    pe.wait_ge(h_lo_ready, 2 * (t - 2) + 2)
                for b in range(2):
                    for k in range(4):
                        last = nc.tensor.transpose(psum[:, 2 * (t % 2) + b, k * P:(k + 1) * P],
                                                   x_in[:, t % 3, (4 * b + k) * P:(4 * b + k + 1) * P], ident[:])
                    last.then_inc(x_turned, 1)

            for t in range(NT):
                turn(t)
                if t == 3:
                    pe.wait_ge(small_in, 16 * SMALL)
                    for c in range(LC):
                        last = nc.tensor.transpose(psum[:, 4, c * ROWS:(c + 1) * ROWS], rows[:, c * P:(c + 1) * P],
                                                   ident[0:ROWS, 0:ROWS])
                    last.then_inc(rows_turned, 1)
            pe.wait_ge(wf_ready, 1)
            pe.wait_ge(h_lo_ready, 2 * NT)
            for g in range(G):
                n = slice(g * GN, (g + 1) * GN)
                split_product(psum[0:H, 5 + g, 0:GN], lambda k: wf_hi[:, k, :], lambda k: wf_lo[:, k, :],
                              lambda k: h_hi[:, k, n], lambda k: h_lo[:, k, n], KC).then_inc(f_done, 1)
            pe.wait_ge(f_copied, G)
            pe.wait_ge(params_copied, 1)
            for t in range(NT):
                last = nc.tensor.transpose(psum[:, 4, 256 + t * H:256 + (t + 1) * H], f_rows[:, t * P:(t + 1) * P],
                                           ident[0:H, 0:H])
            last.then_inc(f_turned, 1)

            def chunk(c, last_chunk):
                for u in range(2):
                    pe.wait_ge(w_lo, 2 * c + u + 1)
                    if u == 1 and last_chunk:
                        pe.wait_ge(c_read, 1)
                    for g in range(G):
                        n = slice(g * GN, (g + 1) * GN)
                        split_product(psum[:, 3 * u + g, 0:GN], lambda k: wl_hi[:, u, k, :], lambda k: wl_lo[:, u, k, :],
                                      lambda k: h_hi[:, k, n], lambda k: h_lo[:, k, n], KC).then_inc(proj_done, 1)
                pe.wait_ge(xc_ready, c + 1)
                pe.wait_ge(gw_in, 64 * c + 64)
                for m in range(6):
                    g = m % 3
                    if m >= 2:
                        pe.wait_ge(gate_read, 6 * c + m - 1)
                    nc.tensor.matmul(psum[:, 6 + m % 2, 0:GN], gate_w[:, m // 3, :], xc[:, g * GN:(g + 1) * GN],
                                     start=True, stop=True).then_inc(gate_done, 1)

            pe.wait_ge(l_abs, 1)
            with pe.Fori(0, LC - 1) as c:
                chunk(c, False)
            pe.wait_ge(gate_read, 6 * (LC - 1))
            pe.wait_ge(logf_ready, 1)
            for t in range(SEQ // P):
                nc.tensor.transpose(psum[0:H, 3 + t // 4, (t % 4) * P:(t % 4 + 1) * P], l_f[:, t * H:(t + 1) * H], ident[:])
            for kt in range(KP):
                last = nc.tensor.transpose(psum[0:64, 5, kt * P:(kt + 1) * P], cl[:, kt, :], ident[:])
            last.then_inc(c_turned, 1)
            pe.wait_ge(c_own_ready, 1)
            nc.tensor.matmul(psum[0:64, 6, 0:P], lf_own[:].rearrange("p b h -> p (b h)"), ident[:],
                             start=True, stop=True).then_inc(c_turned, 1)
            chunk(LC - 1, True)
            pe.wait_ge(gate_read, 6 * LC)

            def pair_pe(p):
                pe.wait_ge(w_lo, 2 * LC + 4 * p + 4)

                def turn_qk(t):
                    pe.wait_ge(qk_ready, NT * p + t + 1)
                    if t == NT - 1:
                        pe.wait_ge(q_done, 3 * p + 1)
                        pe.wait_ge(k_done, 3 * p + 1)
                    at = slice((t % 4) * P, (t % 4 + 1) * P)
                    nc.tensor.transpose(psum[:, QB[t // 4], at], qk[:, t % 3, 0:P], ident[:])
                    nc.tensor.transpose(psum[:, KB[t // 4], at], qk[:, t % 3, P:2 * P], ident[:]).then_inc(qk_turned, 1)

                for t in range(NT):
                    if t == 2:
                        pe.wait_ge(s_out, p + 1)
                    if t >= 3:
                        pe.wait_ge(qk_ready, NT * p + t - 2)
                        pe.wait_ge(v_done, NT * p + t - 2)
                    n = slice(t * P, (t + 1) * P)
                    split_product(psum[:, PB[t % 3], 0:PW3], lambda k: h_hi[:, k, n], lambda k: h_lo[:, k, n],
                                  lambda k: wp_hi[:, k, :], lambda k: wp_lo[:, k, :], KC).then_inc(pair_proj, 1)
                    if t >= 2:
                        turn_qk(t - 2)
                turn_qk(NT - 2)

                def score(s):
                    t, hp = step_of(s)
                    nk = t + 1
                    if s >= 2:
                        pe.wait_ge(exp_done, 16 * p + s - 1)
                    r = slice(hp * DH, (hp + 1) * DH)
                    for part in range((nk + 3) // 4):
                        n = min(nk - 4 * part, 4) * P
                        out = psum[:, SB[s % 2] + part, 0:n]
                        keys = slice(part * SPAN, part * SPAN + n)
                        nc.tensor.matmul(out, e_head[:, bass.ds(2 * p + hp, 1), :].rearrange("p a m -> p (a m)"),
                                         c_prompt[:, keys], start=True, stop=False)
                        if part == t // 4:
                            nc.tensor.matmul(psum[:, SB[s % 2] + part, n - P:n], ident_b[:], cmask[:],
                                             start=False, stop=False)
                        last = nc.tensor.matmul(out, qt[r, t * P:(t + 1) * P], kt_all[r, keys], start=False, stop=True)
                    last.then_inc(scores, 1)

                def turn_probs(s):
                    pe.wait_ge(exp_done, 16 * p + s + 1)
                    if s >= 1:
                        pe.wait_ge(pt_a, 16 * p + s)
                    if s >= 9:
                        pe.wait_ge(pt_b, 8 * p + s - 8)
                    for kt in range(step_of(s)[0] + 1):
                        last = nc.tensor.transpose(psum[:, 2 + kt // 4, (kt % 4) * P:(kt % 4 + 1) * P],
                                                   probs[:, s % 2, kt * P:(kt + 1) * P], ident[:])
                    last.then_inc(p_turned, 1)

                def values(s):
                    t, hp = step_of(s)
                    r = slice(hp * DH, (hp + 1) * DH)
                    pe.wait_ge(pt_a, 16 * p + s + 1)
                    if s >= 8:
                        pe.wait_ge(pt_b, 8 * p + s - 7)
                    if t >= 2:
                        pe.wait_ge(o_done, 8 * p + t - 1)
                    for kt in range(t + 1):
                        last = nc.tensor.matmul(psum[:, t % 2, r], pts[:, 2 * (s % 2) + kt // 4, (kt % 4) * P:(kt % 4 + 1) * P],
                                                vt[:, kt, r], start=kt == 0, stop=kt == t)
                    last.then_inc(pv_done, 1)

                def turn_out(t):
                    pe.wait_ge(o_scaled, 8 * p + t + 1)
                    nc.tensor.transpose(psum[:, t % 2, P:2 * P], o_tok[:, t % 2, :], ident[:]).then_inc(o_turned, 1)

                pe.wait_ge(v_done, NT * p + NT - 2)
                pe.wait_ge(q_done, 3 * p + 1)
                pe.wait_ge(k_done, 3 * p + 1)
                score(0)
                turn_qk(NT - 1)
                pe.wait_ge(q_done, 3 * p + 2)
                pe.wait_ge(k_done, 3 * p + 2)
                for s in range(16):
                    if s < 15:
                        score(s + 1)
                    if s == 0:
                        pe.wait_ge(q_done, 3 * p + 3)
                        pe.wait_ge(k_done, 3 * p + 3)
                        pe.wait_ge(v_done, NT * p + NT)
                    turn_probs(s)
                    if s >= 1:
                        values(s - 1)
                    if s >= 3 and s % 2 == 1:
                        turn_out((s - 3) // 2)
                values(15)

                pe.wait_ge(q_blocks_ready, 2 * p + 2)
                pe.wait_ge(pt_a, 16 * p + 16)
                pe.wait_ge(pt_b, 8 * p + 8)
                pe.wait_ge(exp_done, 16 * p + 16)

                def turn_past(b):
                    pe.wait_ge(kc_in[b % 2], 64 * p + 16 * (b // 2) + 16)
                    if b >= 2:
                        pe.wait_ge((kts_a, kts_b)[b % 2], 4 * p + b // 2)
                    for kt in range(KP):
                        last = nc.tensor.transpose(psum[:, 2 + b % 2, kt * P:(kt + 1) * P], k_c[:, b % 2, kt, :], ident[:])
                    last.then_inc(kc_turned, 1)

                def score_stream(b):
                    g, r = b // 4, slice((b % 4) * 32, (b % 4 + 1) * 32)
                    past, new = psum[:, SB[g], 0:PAST], psum[:, SB[g] + 1, 0:P]
                    if b % 4 == 0:
                        rows_of = e_row[:, bass.ds(2 * p + g, 1), :].rearrange("p a m -> p (a m)")
                        nc.tensor.matmul(past, rows_of, c_past[:, 0, 0:PAST], start=True, stop=False)
                        nc.tensor.matmul(past, rows_of, c_past[:, 1, 0:PAST], start=False, stop=False)
                        nc.tensor.matmul(new, rows_of, c_past[:, 0, PAST:], start=True, stop=False)
                        nc.tensor.matmul(new, rows_of, c_past[:, 1, PAST:], start=False, stop=False)
                        nc.tensor.matmul(new, ident_b[:], smask[:, g, :], start=False, stop=False)
                    pe.wait_ge((kts_a, kts_b)[b % 2], 4 * p + b // 2 + 1)
                    q = q_blocks[:, b, :, :].rearrange("p h q -> p (h q)")
                    nc.tensor.matmul(psum[r, SB[g], 0:PAST], q, pts[:, 2 + b % 2, :], start=False, stop=True)
                    last = nc.tensor.matmul(psum[r, SB[g] + 1, 0:P], q, kt_all[:, SEQ:], start=False, stop=True)
                    if b % 4 == 3:
                        last.then_inc(s_scores, 1)

                turn_past(0)
                for b in range(DEC_B):
                    if b < DEC_B - 1:
                        turn_past(b + 1)
                    if b == 0:
                        turn_out(7)
                    score_stream(b)
                pe.wait_ge(o_done, 8 * p + 8)

                def turn_stream_probs(g):
                    pe.wait_ge(s_probs, 2 * p + g + 1)
                    for kt in range(KP):
                        nc.tensor.transpose(psum[:, 2, kt * P:(kt + 1) * P], probs[:, g, kt * P:(kt + 1) * P], ident[:])
                    nc.tensor.transpose(psum[:, 3, 0:P], probs[:, g, PAST:KEYS], ident[:]).then_inc(s_turned, 1)

                turn_stream_probs(0)
                for g in range(2):
                    pe.wait_ge(s_ptb, 2 * p + g + 1)
                    pe.wait_ge(s_pta, 2 * p + g + 1)
                    nc.tensor.matmul(psum[:, g, 0:P], vt[:, NT - 1, :], pts[:, 2 * g + 1, 0:P], start=True, stop=False)
                    for b in range(4):
                        if g == 0 and b == 2:
                            turn_stream_probs(1)
                        pe.wait_ge(vc_in[b], 32 * p + 16 * g + 16)
                        for kt in range(KP):
                            last = nc.tensor.matmul(psum[:, g, b * 32:(b + 1) * 32], v_c[:, b, kt, :],
                                                    pts[:, 2 * g, kt * P + b * 32:kt * P + (b + 1) * 32],
                                                    start=False, stop=b == 3 and kt == KP - 1)
                    last.then_inc(s_pv, 1)

            with pe.Fori(0, PAIRS) as p:
                pair_pe(p)

            def tile(t):
                return slice(t * P, (t + 1) * P)

            def sums(t):
                pe.wait_ge(mix_ssq, t + 1)
                if t >= 1:
                    pe.wait_ge(mix_ms, t)
                for a in range(2):
                    last = nc.tensor.matmul(psum[:, 6, a:a + 1], ssq[:, a, :], ones_col[:], start=True, stop=True)
                last.then_inc(mix_sums, 1)

            def turn_h2(t):
                pe.wait_ge(h2_ready, t + 1)
                if t >= 1:
                    pe.wait_ge(h2_lo, 2 * t)
                for b in range(2):
                    for k in range(4):
                        last = nc.tensor.transpose(psum[:, 4 + b, k * P:(k + 1) * P], x_e[:, t % 2, 4 * b + k, :], ident[:])
                    last.then_inc(h2_turned, 1)

            pe.wait_ge(s_out, PAIRS + 1)
            for c in range(LC):
                last = nc.tensor.transpose(psum[0:36, 7, c * P:(c + 1) * P], h_keep[:, c, :], ident[:])
            last.then_inc(kept_turned, 1)
            sums(0)
            sums(1)
            for t in range(NT):
                pe.wait_ge(mix_lo, t + 1)
                for half in range(2):
                    if t >= 1:
                        pe.wait_ge(x1_ready, 2 * t - 1 + half)
                    for part in range(2):
                        if t == 0 and half == 0:
                            pe.wait_ge(w_lo, V_OUT + 4 * part + 4)
                        n = slice(half * SPAN, (half + 1) * SPAN)
                        last = split_product(psum[:, 2 * half + part, :],
                                             lambda k: h_hi[:, 4 * part + k, tile(t)], lambda k: h_lo[:, 4 * part + k, tile(t)],
                                             lambda k: wo_hi[:, 4 * part + k, n], lambda k: wo_lo[:, 4 * part + k, n], 4)
                    last.then_inc(out_done, 1)
                if t < NT - 2:
                    sums(t + 2)
                if t >= 1:
                    turn_h2(t - 1)
            def mlp_up(b, par, lo_ready, first=False):
                for c in range(2):
                    pe.wait_ge(w_lo, lo_ready + c)
                    for g in range(G):
                        m = 3 * c + g
                        if not (first and m < 4):
                            pe.wait_ge(up_read, 6 * b + m - 3)
                        if first and m == 1:
                            turn_h2(NT - 1)
                        if first and m < G:
                            pe.wait_ge(h2_lo, 2 * (g * GN + GN) // P)
                        n = slice(g * GN, (g + 1) * GN)
                        split_product(psum[:, up_bank(par, m), 0:GN], lambda k: wu_hi[:, c, k, :], lambda k: wu_lo[:, c, k, :],
                                      lambda k: h_hi[:, k, n], lambda k: h_lo[:, k, n], KC).then_inc(up_done, 1)

            def mlp_down(i, par, lo_ready):
                pe.wait_ge(u_ready, 6 * i + 6)
                pe.wait_ge(w_lo, lo_ready)
                for t in range(NT):
                    for half in range(2):
                        pe.wait_ge(y_added, 2 * NT * i + 2 * t + half + 1)
                        n = slice(half * SPAN, (half + 1) * SPAN)
                        split_product(psum[:, 4 + 2 * (t % 2) + half, :],
                                      lambda k: u_hi[:, par, k, tile(t)], lambda k: u_lo[:, par, k, tile(t)],
                                      lambda k: wd_hi[:, k, n], lambda k: wd_lo[:, k, n], 2).then_inc(down_done, 1)

            pe.wait_ge(kept_copied, 1)
            pe.wait_ge(x1_ready, 2 * NT - 1)
            mlp_up(0, 0, V_MLP + 1, True)
            with pe.Fori(0, (MLP_STEPS - 1) // 2) as j:
                for o in range(2):
                    i = 2 * j + o
                    mlp_up(i + 1, (o + 1) % 2, V_MLP + 4 * i + 3)
                    mlp_down(i, o, V_MLP + 4 * i + 6)
            mlp_up(NFB - 1, (NFB - 1) % 2, V_MLP + 4 * (NFB - 2) + 3)
            mlp_down(NFB - 2, (NFB - 2) % 2, V_MLP + 4 * (NFB - 2) + 6)
            mlp_down(NFB - 1, (NFB - 1) % 2, V_MLP + 4 * (NFB - 1) + 4)
    ctx.close()


_INS = ["x_prompt", "x_sample", "cache_k", "cache_v", "cache_logf", "state_h", "state_conv", "ln1", "w_in", "b_f",
        "q_gain", "k_gain", "conv_w", "conv_b", "w_gate_a", "b_gate_a", "w_gate_x", "b_gate_x", "lru_lambda",
        "g_attn_out", "g_lru_out", "w_out", "ln2", "w_up", "w_down"]
_OUTS = [(1, SEQ, D), (DEC_B, DEC_T, D), (1, 1, SEQ, H, DH), (1, 1, SEQ, H, DH), (1, 1, SEQ, H), (1, 1, LW),
         (1, 1, CW - 1, LW), (1, DEC_B, DEC_T, H, DH), (1, DEC_B, DEC_T, H, DH), (1, DEC_B, DEC_T, H),
         (1, DEC_B, LW), (1, DEC_B, CW - 1, LW)]


def kernel(**inputs):
    from concourse import bacc
    from concourse.bass_utils import run_bass_kernel_spmd

    arrays = {f"in_{name}_dram": np.ascontiguousarray(np.asarray(inputs[name])) for name in _INS}
    nc = bacc.Bacc("TRN2", target_bir_lowering=False, num_devices=1)
    ins = [nc.dram_tensor(f"in_{name}_dram", list(arrays[f"in_{name}_dram"].shape), F32, kind="ExternalInput")
           for name in _INS]
    outs = [nc.dram_tensor(f"out_{i}_dram", list(shape), F32, kind="ExternalOutput") for i, shape in enumerate(_OUTS)]
    streaming_step(nc, *[t.ap() for t in ins], *[t.ap() for t in outs])
    nc.compile()
    results = run_bass_kernel_spmd(nc, [arrays], core_ids=[0]).results[0]
    return tuple(np.asarray(results[f"out_{i}_dram"]) for i in range(len(_OUTS)))
```
